# Optimizing a Trainium2 kernel written in Bass

```python
import math, functools
import jax, jax.numpy as jnp
from jax import lax
import numpy as np

D_MODEL = 1024
BATCH = 1
SEQ = 256
DEPTH = 2
DEC_BATCH = 8
DEC_SEQ = 4
PAST_LEN = 2048
PAGE_SIZE = 128

SSD_HEAD_DIM = 64
SSD_INNER = D_MODEL
SSD_HEADS = SSD_INNER // SSD_HEAD_DIM
SSD_GROUPS = 2
SSD_HPG = SSD_HEADS // SSD_GROUPS
SSD_STATE = 128
SSD_CONV = 4
SSD_CHUNK = 128
SSD_CONV_DIM = SSD_INNER + 2 * SSD_GROUPS * SSD_STATE
SSD_IN = SSD_INNER + SSD_CONV_DIM + SSD_HEADS

RWKV_HEAD_DIM = 64
RWKV_DIM = D_MODEL
RWKV_HEADS = RWKV_DIM // RWKV_HEAD_DIM
RWKV_DECAY_LORA = 64
RWKV_A_LORA = 64
RWKV_GATE_LORA = 128
RWKV_IN = 3 * RWKV_DIM + RWKV_DECAY_LORA + RWKV_A_LORA + RWKV_GATE_LORA
RWKV_LN_EPS = 64e-5

MLA_HEADS = 8
MLA_NOPE = 128
MLA_ROPE = 64
MLA_QK = MLA_NOPE + MLA_ROPE
MLA_V = 128
MLA_Q_RANK = 512
MLA_KV_RANK = 256
MLA_IN = MLA_Q_RANK + MLA_KV_RANK + MLA_ROPE
MLA_OUT = MLA_HEADS * MLA_V
ROPE_BASE = 10000.0
Q_BLOCK = 128

IN_DIM = SSD_IN + RWKV_IN + MLA_IN
N_BRANCH = 3

D_FF = 2816
FFN_CONV = 3
NORM_EPS = 1e-6

kernel_name = 'hybrid_ssd_rwkv7_mla_convffn_step'

def rmsnorm(x, g, eps=NORM_EPS):
    xf = x.astype(jnp.float32)
    y = xf * lax.rsqrt(jnp.mean(xf * xf, axis=-1, keepdims=True) + eps)
    return (y * g.astype(jnp.float32)).astype(x.dtype)

def causal_dwconv(u, buf, w, b):
    k_w = w.shape[0]
    t = u.shape[1]
    full = jnp.concatenate([buf.astype(u.dtype), u], axis=1)
    out = full[:, 0:t] * w[0]
    for j in range(1, k_w):
        out = out + full[:, j:j + t] * w[j]
    return out + b, full[:, t:]

def rope(x, pos):
    half = x.shape[-1] // 2
    inv = ROPE_BASE ** (-jnp.arange(half, dtype=jnp.float32) / half)
    ang = pos.astype(jnp.float32)[:, None] * inv[None, :]
    shape = (ang.shape[0],) + (1,) * (x.ndim - 3) + (half,)
    cos = jnp.cos(ang).reshape(shape)
    sin = jnp.sin(ang).reshape(shape)
    xf = x.astype(jnp.float32)
    x1, x2 = xf[..., :half], xf[..., half:]
    return jnp.concatenate([x1 * cos - x2 * sin, x1 * sin + x2 * cos], axis=-1).astype(x.dtype)

def segsum(a):
    n = a.shape[-1]
    cs = jnp.cumsum(a, axis=-1)
    diff = cs[..., :, None] - cs[..., None, :]
    return jnp.where(jnp.tril(jnp.ones((n, n), bool)), diff, -jnp.inf)

def ssd_scan(x, dt, a, bmat, cmat, h0, chunk):
    f32 = jnp.float32
    b, t, g, j, p = x.shape
    n = bmat.shape[-1]
    nc = t // chunk
    xd = (x.astype(f32) * dt[..., None]).reshape(b, nc, chunk, g, j, p)
    da = jnp.moveaxis((dt * a).reshape(b, nc, chunk, g, j), 2, -1)
    bm = bmat.astype(f32).reshape(b, nc, chunk, g, n)
    cm = cmat.astype(f32).reshape(b, nc, chunk, g, n)
    cs = jnp.cumsum(da, axis=-1)
    lmat = jnp.exp(segsum(da))
    cb = jnp.einsum('bclgn,bcsgn->bcgls', cm, bm)
    y_diag = jnp.einsum('bcgjls,bcsgjp->bclgjp', cb[:, :, :, None] * lmat, xd)
    decay_to_end = jnp.exp(cs[..., -1:] - cs)
    states = jnp.einsum('bclgn,bcgjl,bclgjp->bcgjpn', bm, decay_to_end, xd)
    chunk_decay = jnp.exp(cs[..., -1])

    def step(h, inp):
        s, d = inp
        return h * d[..., None, None] + s, h

    h_fin, h_in = lax.scan(step, h0, (jnp.moveaxis(states, 1, 0), jnp.moveaxis(chunk_decay, 1, 0)))
    h_in = jnp.moveaxis(h_in, 0, 1)
    y_off = jnp.einsum('bclgn,bcgjpn,bcgjl->bclgjp', cm, h_in, jnp.exp(cs))
    return (y_diag + y_off).reshape(b, t, g, j, p), h_fin

def ssd_mixer(u, conv_buf, h0, conv_w, conv_b, dt_bias, a_log, d_skip, norm_g):
    f32 = jnp.float32
    b, t, _ = u.shape
    z = u[..., :SSD_INNER]
    xbc, conv_buf = causal_dwconv(u[..., SSD_INNER:SSD_INNER + SSD_CONV_DIM], conv_buf, conv_w, conv_b)
    xbc = jax.nn.silu(xbc)
    gn = SSD_GROUPS * SSD_STATE
    xs = xbc[..., :SSD_INNER].reshape(b, t, SSD_GROUPS, SSD_HPG, SSD_HEAD_DIM)
    bm = xbc[..., SSD_INNER:SSD_INNER + gn].reshape(b, t, SSD_GROUPS, SSD_STATE)
    cm = xbc[..., SSD_INNER + gn:].reshape(b, t, SSD_GROUPS, SSD_STATE)
    dt = jax.nn.softplus(u[..., SSD_INNER + SSD_CONV_DIM:].astype(f32) + dt_bias.astype(f32))
    dt = dt.reshape(b, t, SSD_GROUPS, SSD_HPG)
    a = -jnp.exp(a_log.astype(f32)).reshape(SSD_GROUPS, SSD_HPG)
    chunk = SSD_CHUNK if t % SSD_CHUNK == 0 else t
    h0 = h0.astype(f32).reshape(b, SSD_GROUPS, SSD_HPG, SSD_HEAD_DIM, SSD_STATE)
    y, h = ssd_scan(xs, dt, a, bm, cm, h0, chunk)
    y = y + d_skip.astype(f32).reshape(SSD_GROUPS, SSD_HPG, 1) * xs.astype(f32)
    y = y.reshape(b, t, SSD_INNER) * jax.nn.silu(z.astype(f32))
    y = rmsnorm(y.reshape(b, t, SSD_GROUPS, SSD_INNER // SSD_GROUPS), norm_g.reshape(SSD_GROUPS, -1))
    return (y.reshape(b, t, SSD_INNER).astype(u.dtype), conv_buf,
            h.reshape(b, SSD_HEADS, SSD_HEAD_DIM, SSD_STATE))

def rwkv_mixer(u, shift_buf, s0, mu, w0, w_up, a0, a_up, g_up, k_k, k_a, r_k, ln_g, ln_b):
    f32 = jnp.float32
    b, t, _ = u.shape
    d = RWKV_DIM
    prev = jnp.concatenate([shift_buf[:, None, :].astype(u.dtype), u[:, :-1]], axis=1)
    f = (u + mu * (prev - u)).astype(f32)
    new_buf = u[:, -1]
    r, k, v = f[..., :d], f[..., d:2 * d], f[..., 2 * d:3 * d]
    o1 = 3 * d + RWKV_DECAY_LORA
    o2 = o1 + RWKV_A_LORA
    w_lo, a_lo, g_lo = f[..., 3 * d:o1], f[..., o1:o2], f[..., o2:]
    w_log = -jax.nn.softplus(-(w0 + jnp.tanh(w_lo) @ w_up)) - 0.5
    decay = jnp.exp(-jnp.exp(w_log))
    a = jax.nn.sigmoid(a0 + a_lo @ a_up)
    g = jax.nn.sigmoid(g_lo) @ g_up

    def heads(z):
        return z.reshape(b, t, RWKV_HEADS, RWKV_HEAD_DIM)

    kk = heads(k * k_k)
    kk = kk / jnp.maximum(jnp.sqrt(jnp.sum(kk * kk, axis=-1, keepdims=True)), 1e-12)
    k = k * (1.0 + (a - 1.0) * k_a)
    rh, kh, vh, wh, ah = heads(r), heads(k), heads(v), heads(decay), heads(a)

    def step(s, inp):
        r_t, w_t, k_t, v_t, kk_t, a_t = inp
        sa = jnp.einsum('bhvk,bhk->bhv', s, -kk_t)
        s = (s * w_t[:, :, None, :] + sa[..., None] * (kk_t * a_t)[:, :, None, :]
             + v_t[..., None] * k_t[:, :, None, :])
        return s, jnp.einsum('bhvk,bhk->bhv', s, r_t)

    def tm(z):
        return jnp.moveaxis(z, 1, 0)

    s_fin, y = lax.scan(step, s0.astype(f32), (tm(rh), tm(wh), tm(kh), tm(vh), tm(kk), tm(ah)))
    y = jnp.moveaxis(y, 0, 1)
    mean = jnp.mean(y, axis=-1, keepdims=True)
    var = jnp.mean(jnp.square(y - mean), axis=-1, keepdims=True)
    y = ((y - mean) * lax.rsqrt(var + RWKV_LN_EPS)).reshape(b, t, d) * ln_g + ln_b
    bonus = jnp.sum(rh * kh * r_k, axis=-1, keepdims=True) * vh
    out = (y + bonus.reshape(b, t, d)) * g
    return out.astype(u.dtype), new_buf, s_fin

def mla_queries(cq, pos, q_a_g, w_q_b, q_norm_g):
    q = jnp.einsum('btr,rhe->bthe', rmsnorm(cq, q_a_g), w_q_b)
    q = jnp.concatenate([q[..., :MLA_NOPE], rope(q[..., MLA_NOPE:], pos)], axis=-1)
    return rmsnorm(q, q_norm_g)

def mla_keys(ckv, kpe, w_kb, k_norm_g):
    kn = jnp.einsum('blr,rhe->blhe', ckv, w_kb)
    kp = jnp.broadcast_to(kpe[:, :, None, :], kn.shape[:-1] + (MLA_ROPE,)).astype(kn.dtype)
    return rmsnorm(jnp.concatenate([kn, kp], axis=-1), k_norm_g)

def block_causal_attention(q, k, v):
    b, s, h, e = q.shape
    nb = s // Q_BLOCK
    scale = e ** -0.5
    q_blocks = jnp.moveaxis(q.reshape(b, nb, Q_BLOCK, h, e), 1, 0)
    k_pos = jnp.arange(s)

    def one_block(args):
        qi, start = args
        sc = jnp.einsum('bqhe,bkhe->bhqk', qi, k).astype(jnp.float32) * scale
        q_pos = start + jnp.arange(Q_BLOCK)
        sc = jnp.where(k_pos[None, :] <= q_pos[:, None], sc, -jnp.inf)
        pr = jax.nn.softmax(sc, axis=-1).astype(v.dtype)
        return jnp.einsum('bhqk,bkhv->bqhv', pr, v)

    o = lax.map(one_block, (q_blocks, jnp.arange(nb) * Q_BLOCK))
    return jnp.moveaxis(o, 0, 1).reshape(b, s, h, v.shape[-1])

def prompt_mla(q, ckv, kpe, p):
    k = mla_keys(ckv, kpe, p['mla_w_kb'], p['mla_k_norm_g'])
    v = jnp.einsum('blr,rhv->blhv', ckv, p['mla_w_vb'])
    return block_causal_attention(q, k, v)

def sample_mla(q, ckv, kpe, p, lat_pool, rope_pool, page_table):
    f32 = jnp.float32
    b, t, h, e = q.shape
    scale = e ** -0.5

    def scores(c, kr):
        k = mla_keys(c, kr, p['mla_w_kb'], p['mla_k_norm_g'])
        return jnp.einsum('bqhe,blhe->bhql', q, k).astype(f32) * scale

    def update(carry, sc, c):
        m, l, acc = carry
        m_new = jnp.maximum(m, jnp.max(sc, axis=-1))
        corr = jnp.exp(m - m_new)
        pr = jnp.exp(sc - m_new[..., None])
        l = l * corr + jnp.sum(pr, axis=-1)
        acc = acc * corr[..., None] + jnp.einsum('bhql,blr->bhqr', pr, c.astype(f32))
        return (m_new, l, acc)

    def page_step(carry, phys):
        c = lat_pool[phys]
        kr = rope_pool[phys]
        return update(carry, scores(c, kr), c), None

    init = (jnp.full((b, h, t), -jnp.inf, f32), jnp.zeros((b, h, t), f32),
            jnp.zeros((b, h, t, MLA_KV_RANK), f32))
    carry, _ = lax.scan(page_step, init, page_table.T)
    sc = jnp.where(jnp.tril(jnp.ones((t, t), bool)), scores(ckv, kpe), -jnp.inf)
    m, l, acc = update(carry, sc, ckv)
    o_lat = (acc / l[..., None]).astype(ckv.dtype)
    return jnp.einsum('bhqr,rhv->bqhv', o_lat, p['mla_w_vb'])

def trunk_layer(x, pos, states, attend, p):
    ssd_buf, ssd_h, rwkv_buf, rwkv_s, ffn_buf = states
    b, t, _ = x.shape
    h = rmsnorm(x, p['norm_mix_g'])
    u = h @ p['w_in']
    u_ssd = u[..., :SSD_IN]
    u_rwkv = u[..., SSD_IN:SSD_IN + RWKV_IN]
    u_mla = u[..., SSD_IN + RWKV_IN:]
    o_ssd, ssd_buf, ssd_h = ssd_mixer(u_ssd, ssd_buf, ssd_h, p['ssd_conv_w'], p['ssd_conv_b'],
                                      p['ssd_dt_bias'], p['ssd_a_log'], p['ssd_d'], p['ssd_norm_g'])
    o_rwkv, rwkv_buf, rwkv_s = rwkv_mixer(u_rwkv, rwkv_buf, rwkv_s, p['rwkv_shift_mu'], p['rwkv_w0'],
                                          p['rwkv_w_up'], p['rwkv_a0'], p['rwkv_a_up'], p['rwkv_g_up'],
                                          p['rwkv_k_k'], p['rwkv_k_a'], p['rwkv_r_k'],
                                          p['rwkv_ln_g'], p['rwkv_ln_b'])
    q = mla_queries(u_mla[..., :MLA_Q_RANK], pos, p['mla_q_a_g'], p['mla_w_q_b'], p['mla_q_norm_g'])
    ckv = rmsnorm(u_mla[..., MLA_Q_RANK:MLA_Q_RANK + MLA_KV_RANK], p['mla_kv_a_g'])
    kpe = rope(u_mla[..., MLA_Q_RANK + MLA_KV_RANK:], pos)
    o_mla = attend(q, ckv, kpe, p).reshape(b, t, MLA_OUT)
    gates = jax.nn.sigmoid(h @ p['w_gate'] + p['b_gate']).reshape(b, t, N_BRANCH, D_MODEL)
    merged = (gates[:, :, 0] * (o_ssd @ p['w_o_ssd'])
              + gates[:, :, 1] * (o_rwkv @ p['w_o_rwkv'])
              + gates[:, :, 2] * (o_mla @ p['w_o_mla']))
    x = x + merged @ p['w_out']
    h2 = rmsnorm(x, p['norm_ffn_g'])
    up, ffn_buf = causal_dwconv(h2 @ p['ffn_w_up'], ffn_buf, p['ffn_conv_w'], p['ffn_conv_b'])
    x = x + (jax.nn.silu(up[..., :D_FF]) * up[..., D_FF:]) @ p['ffn_w_down']
    return x, (ssd_buf, ssd_h, rwkv_buf, rwkv_s, ffn_buf), ckv, kpe

def setup_inputs(seed: int = 0) -> dict:
    key = jax.random.key(seed)
    keys = iter(jax.random.split(key, 64))
    f32 = jnp.float32

    def nrm(shape, scale=1.0):
        return jax.random.normal(next(keys), shape, f32) * scale

    def gain(shape):
        return 1.0 + nrm(shape, 0.02)

    def unif(shape, lo, hi):
        return jax.random.uniform(next(keys), shape, f32, lo, hi)

    n_pages = PAST_LEN // PAGE_SIZE
    n_used = DEC_BATCH * n_pages
    n_pool = n_used + max(1, n_used // 4)
    L = DEPTH
    x_prompt = nrm((BATCH, SEQ, D_MODEL))
    x_sample = nrm((DEC_BATCH, DEC_SEQ, D_MODEL))
    cache_kv_latent = nrm((L, n_pool, PAGE_SIZE, MLA_KV_RANK))
    cache_k_rope = nrm((L, n_pool, PAGE_SIZE, MLA_ROPE))
    page_table = jax.random.permutation(next(keys), n_pool)[:n_used].reshape(DEC_BATCH, n_pages).astype(jnp.int32)
    dt_init = jnp.exp(unif((L, SSD_HEADS), math.log(1e-3), math.log(1e-1)))
    return {
        'x_prompt': x_prompt,
        'x_sample': x_sample,
        'cache_kv_latent': cache_kv_latent,
        'cache_k_rope': cache_k_rope,
        'page_table': page_table,
        'state_ssm': nrm((L, DEC_BATCH, SSD_HEADS, SSD_HEAD_DIM, SSD_STATE), 0.5),
        'state_ssm_conv': nrm((L, DEC_BATCH, SSD_CONV - 1, SSD_CONV_DIM)),
        'state_rwkv': nrm((L, DEC_BATCH, RWKV_HEADS, RWKV_HEAD_DIM, RWKV_HEAD_DIM), 0.5),
        'state_rwkv_shift': nrm((L, DEC_BATCH, RWKV_IN)),
        'state_ffn_conv': nrm((L, DEC_BATCH, FFN_CONV - 1, 2 * D_FF)),
        'norm_mix_g': gain((L, D_MODEL)),
        'w_in': nrm((L, D_MODEL, IN_DIM), D_MODEL ** -0.5),
        'ssd_conv_w': nrm((L, SSD_CONV, SSD_CONV_DIM), SSD_CONV ** -0.5),
        'ssd_conv_b': nrm((L, SSD_CONV_DIM), 0.02),
        'ssd_dt_bias': dt_init + jnp.log(-jnp.expm1(-dt_init)),
        'ssd_a_log': jnp.log(unif((L, SSD_HEADS), 1.0, 16.0)),
        'ssd_d': 1.0 + nrm((L, SSD_HEADS), 0.1),
        'ssd_norm_g': gain((L, SSD_INNER)),
        'rwkv_shift_mu': unif((L, RWKV_IN), 0.0, 1.0),
        'rwkv_w0': nrm((L, RWKV_DIM), 0.5) - 1.0,
        'rwkv_w_up': nrm((L, RWKV_DECAY_LORA, RWKV_DIM), 0.5 * RWKV_DECAY_LORA ** -0.5),
        'rwkv_a0': nrm((L, RWKV_DIM), 0.1),
        'rwkv_a_up': nrm((L, RWKV_A_LORA, RWKV_DIM), 0.5 * RWKV_A_LORA ** -0.5),
        'rwkv_g_up': nrm((L, RWKV_GATE_LORA, RWKV_DIM), RWKV_GATE_LORA ** -0.5),
        'rwkv_k_k': 0.85 + nrm((L, RWKV_DIM), 0.05),
        'rwkv_k_a': 1.0 + nrm((L, RWKV_DIM), 0.05),
        'rwkv_r_k': nrm((L, RWKV_HEADS, RWKV_HEAD_DIM), 0.1),
        'rwkv_ln_g': gain((L, RWKV_DIM)),
        'rwkv_ln_b': nrm((L, RWKV_DIM), 0.02),
        'mla_q_a_g': gain((L, MLA_Q_RANK)),
        'mla_w_q_b': nrm((L, MLA_Q_RANK, MLA_HEADS, MLA_QK), MLA_Q_RANK ** -0.5),
        'mla_kv_a_g': gain((L, MLA_KV_RANK)),
        'mla_w_kb': nrm((L, MLA_KV_RANK, MLA_HEADS, MLA_NOPE), MLA_KV_RANK ** -0.5),
        'mla_w_vb': nrm((L, MLA_KV_RANK, MLA_HEADS, MLA_V), MLA_KV_RANK ** -0.5),
        'mla_q_norm_g': gain((L, MLA_QK)),
        'mla_k_norm_g': gain((L, MLA_QK)),
        'w_gate': nrm((L, D_MODEL, N_BRANCH * D_MODEL), D_MODEL ** -0.5),
        'b_gate': nrm((L, N_BRANCH * D_MODEL), 0.02),
        'w_o_ssd': nrm((L, SSD_INNER, D_MODEL), SSD_INNER ** -0.5),
        'w_o_rwkv': nrm((L, RWKV_DIM, D_MODEL), RWKV_DIM ** -0.5),
        'w_o_mla': nrm((L, MLA_OUT, D_MODEL), MLA_OUT ** -0.5),
        'w_out': nrm((L, D_MODEL, D_MODEL), D_MODEL ** -0.5),
        'norm_ffn_g': gain((L, D_MODEL)),
        'ffn_w_up': nrm((L, D_MODEL, 2 * D_FF), D_MODEL ** -0.5),
        'ffn_conv_w': nrm((L, FFN_CONV, 2 * D_FF), FFN_CONV ** -0.5),
        'ffn_conv_b': nrm((L, 2 * D_FF), 0.02),
        'ffn_w_down': nrm((L, D_FF, D_MODEL), D_FF ** -0.5),
    }

def reference(x_prompt, x_sample, cache_kv_latent, cache_k_rope, page_table, state_ssm, state_ssm_conv,
              state_rwkv, state_rwkv_shift, state_ffn_conv, norm_mix_g, w_in, ssd_conv_w, ssd_conv_b,
              ssd_dt_bias, ssd_a_log, ssd_d, ssd_norm_g, rwkv_shift_mu, rwkv_w0, rwkv_w_up, rwkv_a0,
              rwkv_a_up, rwkv_g_up, rwkv_k_k, rwkv_k_a, rwkv_r_k, rwkv_ln_g, rwkv_ln_b, mla_q_a_g,
              mla_w_q_b, mla_kv_a_g, mla_w_kb, mla_w_vb, mla_q_norm_g, mla_k_norm_g, w_gate, b_gate,
              w_o_ssd, w_o_rwkv, w_o_mla, w_out, norm_ffn_g, ffn_w_up, ffn_conv_w, ffn_conv_b, ffn_w_down):
    f32 = jnp.float32
    act = x_prompt.dtype
    b, s, _ = x_prompt.shape
    bd, td, _ = x_sample.shape
    past_len = page_table.shape[1] * PAGE_SIZE
    pos_p = jnp.arange(s)
    pos_s = past_len + jnp.arange(td)
    xp, xs = x_prompt, x_sample
    new_p = [[] for _ in range(7)]
    new_s = [[] for _ in range(7)]
    for i in range(DEPTH):
        p = dict(norm_mix_g=norm_mix_g[i], w_in=w_in[i], ssd_conv_w=ssd_conv_w[i], ssd_conv_b=ssd_conv_b[i],
                 ssd_dt_bias=ssd_dt_bias[i], ssd_a_log=ssd_a_log[i], ssd_d=ssd_d[i], ssd_norm_g=ssd_norm_g[i],
                 rwkv_shift_mu=rwkv_shift_mu[i], rwkv_w0=rwkv_w0[i], rwkv_w_up=rwkv_w_up[i],
                 rwkv_a0=rwkv_a0[i], rwkv_a_up=rwkv_a_up[i], rwkv_g_up=rwkv_g_up[i], rwkv_k_k=rwkv_k_k[i],
                 rwkv_k_a=rwkv_k_a[i], rwkv_r_k=rwkv_r_k[i], rwkv_ln_g=rwkv_ln_g[i], rwkv_ln_b=rwkv_ln_b[i],
                 mla_q_a_g=mla_q_a_g[i], mla_w_q_b=mla_w_q_b[i], mla_kv_a_g=mla_kv_a_g[i],
                 mla_w_kb=mla_w_kb[i], mla_w_vb=mla_w_vb[i], mla_q_norm_g=mla_q_norm_g[i],
                 mla_k_norm_g=mla_k_norm_g[i], w_gate=w_gate[i], b_gate=b_gate[i], w_o_ssd=w_o_ssd[i],
                 w_o_rwkv=w_o_rwkv[i], w_o_mla=w_o_mla[i], w_out=w_out[i], norm_ffn_g=norm_ffn_g[i],
                 ffn_w_up=ffn_w_up[i], ffn_conv_w=ffn_conv_w[i], ffn_conv_b=ffn_conv_b[i],
                 ffn_w_down=ffn_w_down[i])
        zero_state = (jnp.zeros((b, SSD_CONV - 1, SSD_CONV_DIM), act),
                      jnp.zeros((b, SSD_HEADS, SSD_HEAD_DIM, SSD_STATE), f32),
                      jnp.zeros((b, RWKV_IN), act),
                      jnp.zeros((b, RWKV_HEADS, RWKV_HEAD_DIM, RWKV_HEAD_DIM), f32),
                      jnp.zeros((b, FFN_CONV - 1, 2 * D_FF), act))
        xp, st_p, ckv_p, kpe_p = trunk_layer(xp, pos_p, zero_state, prompt_mla, p)
        sample_attend = functools.partial(sample_mla, lat_pool=cache_kv_latent[i],
                                          rope_pool=cache_k_rope[i], page_table=page_table)
        st_in = (state_ssm_conv[i], state_ssm[i], state_rwkv_shift[i], state_rwkv[i], state_ffn_conv[i])
        xs, st_s, ckv_s, kpe_s = trunk_layer(xs, pos_s, st_in, sample_attend, p)
        for lst, vals in ((new_p, (ckv_p, kpe_p, st_p[1], st_p[0], st_p[3], st_p[2], st_p[4])),
                          (new_s, (ckv_s, kpe_s, st_s[1], st_s[0], st_s[3], st_s[2], st_s[4]))):
            for j in range(7):
                lst[j].append(vals[j])
    p_lat, p_rope, p_ssm, p_ssm_conv, p_rwkv, p_rwkv_shift, p_ffn_conv = [jnp.stack(v, axis=0) for v in new_p]
    s_lat, s_rope, s_ssm, s_ssm_conv, s_rwkv, s_rwkv_shift, s_ffn_conv = [jnp.stack(v, axis=0) for v in new_s]
    return (xp, xs, p_lat, p_rope, p_ssm, p_ssm_conv, p_rwkv, p_rwkv_shift, p_ffn_conv,
            s_lat, s_rope, s_ssm, s_ssm_conv, s_rwkv, s_rwkv_shift, s_ffn_conv)


_drawn_inputs = setup_inputs


def setup_inputs(seed=0):
    import zlib

    import numpy as np

    out = dict(_drawn_inputs(seed))
    spreads = {}
    factors = {'cache_k_rope': 4.373,
     'ssd_norm_g': 3.875,
     'rwkv_k_k': 11.422,
     'rwkv_ln_g': 7.206,
     'rwkv_ln_b': 6.537,
     'mla_q_a_g': 8.0,
     'mla_q_norm_g': 8.0,
     'mla_k_norm_g': 8.0,
     'b_gate': 8.0,
     'ffn_conv_b': 2.971,
     'norm_ffn_g': 2.723}
    for name, (base, spread) in spreads.items():
        noise = np.random.default_rng([zlib.crc32(name.encode()), seed]).standard_normal(out[name].shape)
        drawn = base * np.exp(spread * noise) if base else spread * noise
        out[name] = __import__('jax').numpy.asarray(drawn.astype(out[name].dtype))
    for name, factor in factors.items():
        out[name] = (out[name] * factor).astype(out[name].dtype)
    return out
```

```python
from contextlib import ExitStack

import numpy as np

import concourse.bass as bass
from concourse import mybir

F32 = mybir.dt.float32
I32 = mybir.dt.int32
F32R = mybir.dt.float32r
ALU = mybir.AluOpType
ACT = mybir.ActivationFunctionType
AX = mybir.AxisListType
ds = bass.ds

P = 128
D = 1024
DT = D // P
SEQ = 256
DEPTH = 2
NB = 8
NS = 4
NSAM = NB * NS
T = SEQ + NSAM
TOK = [(0, 128), (128, 128), (SEQ, NSAM)]
PAGES = 16
NPOOL = 160
SSD_HEADS, SSD_GROUPS, SSD_STATE = 16, 2, 128
SSD_CONV_DIM = D + 2 * SSD_GROUPS * SSD_STATE
CT = SSD_CONV_DIM // P
SSD_IN = D + SSD_CONV_DIM + SSD_HEADS
RWKV_IN = 3 * D + 256
RT = RWKV_IN // P
HEADS, NOPE, ROPE, QRANK, KVRANK = 8, 128, 64, 512, 256
QK = NOPE + ROPE
D_FF = 2816
FT = D_FF // P
EPS = 1e-6
RWKV_EPS = 64e-5
OFF_Z, OFF_XBC, OFF_DT = 0, D, D + SSD_CONV_DIM
OFF_RWKV = SSD_IN
OFF_MLA = SSD_IN + RWKV_IN
CH = 64
RING = 3
BANK = 512

PARAM_ROWS = [
    [("norm_mix_g", 8), ("rwkv_shift_mu", 26), ("rwkv_w0", 8), ("rwkv_a0", 8), ("rwkv_k_k", 8),
     ("rwkv_k_a", 8), ("rwkv_r_k", 8), ("rwkv_ln_g", 8), ("rwkv_ln_b", 8), ("b_gate", 24),
     ("norm_ffn_g", 8)],
    [("ssd_conv_w", 48), ("ssd_conv_b", 12), ("ssd_norm_g", 8), ("mla_q_a_g", 4),
     ("mla_kv_a_g", 2), ("ffn_conv_b", 44)],
    [("ffn_conv_w01", 88)],
    [("ffn_conv_w2", 44)],
]
PCOL = {}
for _t, _rows in enumerate(PARAM_ROWS):
    _at = 0
    for _name, _n in _rows:
        PCOL[_name] = (_t * P + _at, _n)
        _at += _n

CONSTS = [("ident", 128), ("ones", 128), ("block64", 128), ("tri", 128), ("tri_after", 128),
          ("segtri", 32), ("segtri_after", 32), ("seg", 8), ("segall", 32),
          ("cmask_le", 128), ("cmask_lt", 128)] + [(f"level{n}", 128) for n in range(6)] \
    + [("keep", 256), ("cos", 96), ("sin", 96), ("eps", 1), ("rwkv_eps", 1), ("causal", 128)]
CCOL = {}
_at = 0
for _name, _n in CONSTS:
    CCOL[_name] = (_at, _n)
    _at += _n
NCONST = _at


def const_array():
    c = np.zeros((P, NCONST), np.float32)

    def put(name, a):
        at, n = CCOL[name]
        a = np.asarray(a, np.float32)
        assert a.shape[1] == n, name
        c[:a.shape[0], at:at + n] = a

    i = np.arange(P)
    a, b = i[:, None], i[None, :]
    put("ident", a == b)
    put("ones", np.ones((P, P)))
    put("block64", a // 64 == b // 64)
    put("tri", a <= b)
    put("tri_after", a > b)
    s, t = i[:NSAM, None], i[None, :NSAM]
    put("segtri", (s // NS == t // NS) & (s <= t))
    put("segtri_after", (s // NS == t // NS) & (s > t))
    put("seg", i[:NSAM, None] // NS == i[None, :NB])
    put("segall", (s // NS == t // NS))
    put("cmask_le", (a // CH == b // CH) & (a <= b))
    put("cmask_lt", (a // CH == b // CH) & (a < b))
    for n in range(6):
        w = 1 << n
        put(f"level{n}", (a // (2 * w) == b // (2 * w)) & (a // w % 2 == 1) & (b // w % 2 == 0))
    put("keep", np.broadcast_to((np.arange(SEQ) % CH != 0)[None], (P, SEQ)))
    inv = np.float32(10000.0) ** (-np.arange(32, dtype=np.float32) / np.float32(32))
    cos, sin = np.zeros((P, 96), np.float32), np.zeros((P, 96), np.float32)
    for n, (first, rows) in enumerate(TOK):
        pos = (first + i[:rows]) if n < 2 else PAGES * P + i[:rows] % NS
        ang = pos.astype(np.float32)[:, None] * inv[None]
        cos[:rows, 32 * n:32 * n + 32], sin[:rows, 32 * n:32 * n + 32] = np.cos(ang), np.sin(ang)
    put("cos", cos)
    put("sin", sin)
    put("eps", np.full((P, 1), EPS))
    put("rwkv_eps", np.full((P, 1), RWKV_EPS))
    m = np.zeros((P, P), np.float32)
    m[:, :128] = np.where(a >= b, 0, -1e30)
    put("causal", m)
    return c


def rounds(eng, n, ring, body):
    full = n // ring
    for r in range(min(ring, n)):
        body(0, r, True)
    if full > 1:
        with eng.Fori(1, full) as i:
            for r in range(ring):
                body(i, r, False)
    if full:
        for r in range(n - full * ring):
            body(full, r, False)


class Chain:

    def __init__(self, eng, sem, base=0):
        self.eng, self.sem, self.base, self.n = eng, sem, base, 0

    def __call__(self, ins):
        self.n += 1
        ins.then_inc(self.sem, 1)
        self.eng.wait_ge(self.sem, self.base + self.n)


class Kit:

    def __init__(self, nc, dram):
        self.nc, self.d = nc, dram

    def col(self, name, j=0, n=None, rows=P):
        at, width = CCOL[name]
        return self.const[0:rows, at + j:at + (width if n is None else j + n)]

    def par(self, name, j=0, n=1):
        at, width = PCOL[name]
        return self.params[:, at + j:at + j + n]

    def ldram(self, name):
        a = self.d[name]
        names = "abcdefg"[:len(a.shape) - 1]
        s = a[ds(self.layer, 1)]
        sp = " ".join(names)
        first = f"(l {names[0]})" if names else "l"
        return s.rearrange(f"l {sp} -> {first} {' '.join(names[1:])}")


class Stage:

    built = [0]

    def __init__(self, nc):
        self.nc = nc
        Stage.built[0] += 1
        self.tag = f"_{Stage.built[0]}"

    def __enter__(self):
        self.ctx = ExitStack()
        self.sems = []
        return self

    def sem(self, name):
        s = self.nc.alloc_semaphore(name + self.tag)
        self.sems.append(s)
        return s

    def sb(self, name, shape, dt=F32):
        return self.ctx.enter_context(self.nc.sbuf_tensor(name + self.tag, shape, dt))

    def ps(self, name, shape, dt=F32):
        return self.ctx.enter_context(self.nc.psum_tensor(name + self.tag, shape, dt))

    def block(self):
        return self.nc.Block(no_gpsimd_drain=True)

    def __exit__(self, *e):
        if e[0] is None:
            nums = sorted(s.num for s in self.sems)
            at = 0
            while at < len(nums):
                end = at
                while end + 1 < len(nums) and nums[end + 1] == nums[end] + 1:
                    end += 1
                self.nc.sync.sem_clear(range(nums[at], nums[end] + 1))
                at = end + 1
            self.nc.all_engine_barrier()
            for s in self.sems:
                self.nc.release_semaphore(s)
        self.ctx.close()


def bc(ap, n):
    return ap.unsqueeze(len(ap.shape)).to_broadcast(list(ap.shape) + [n])


def load_x(nc, k):
    with Stage(nc) as st:
        x_tm = st.sb("x_tm", [P, 3, D])
        banks = st.ps("x_banks", [P, 8, BANK])
        loaded, transposed, copied = st.sem("x_loaded"), st.sem("x_transposed"), st.sem("x_copied")
        with st.block() as block:
            @block.sync
            def _(sp):
                sp.dma_start(k.const[:, :], k.d["const"]).then_inc(loaded, 16)
                sp.dma_start(x_tm[:, 0:2, :], k.d["x_prompt"].rearrange("o (n p) d -> p (o n) d", p=P)).then_inc(loaded, 16)
                sp.dma_start(x_tm[0:NSAM, 2, :], k.d["x_sample"].rearrange("b t d -> (b t) d")).then_inc(loaded, 16)

            @block.tensor
            def _(pe):
                pe.wait_ge(loaded, 48)
                for d in range(DT):
                    for n, (first, rows) in enumerate(TOK):
                        last = nc.tensor.transpose(banks[:, d, first:first + rows],
                                                   x_tm[0:rows, n, d * P:(d + 1) * P], k.col("ident", 0, rows, rows))
                    last.then_inc(transposed, 1)

            @block.vector
            def _(dve):
                for d in range(DT):
                    dve.wait_ge(transposed, d + 1)
                    nc.vector.tensor_copy(k.xT[:, d, :], banks[:, d, 0:T]).then_inc(copied, 1)


def load_params(nc, k):
    with Stage(nc) as st:
        rows = st.sb("param_rows", [P, 4, P])
        shift_rows = st.sb("shift_rows", [NB, RWKV_IN])
        sconv_rows = st.sb("sconv_rows", [NB * 3, SSD_CONV_DIM])
        fconv_rows = st.sb("fconv_rows", [NB * 2, 2 * D_FF])
        banks = st.ps("param_banks", [P, 5, BANK])
        params_in, states_in = st.sem("param_rows_loaded"), st.sem("state_rows_loaded")
        small_in = st.sem("broadcast_rows_loaded")
        transposed, copied = st.sem("param_bank_transposed"), st.sem("params_copied")
        n_dma = sum(len(t) for t in PARAM_ROWS)
        with st.block() as block:
            @block.sync
            def _(sp):
                for t, group in enumerate(PARAM_ROWS):
                    at = 0
                    for name, n in group:
                        if name == "ffn_conv_w01":
                            src = k.ldram("ffn_conv_w")[0:2, :].rearrange("j (t p) -> (j t) p", p=P)
                        elif name == "ffn_conv_w2":
                            src = k.ldram("ffn_conv_w")[2:3, :].rearrange("j (t p) -> (j t) p", p=P)
                        elif name == "ssd_conv_w":
                            src = k.ldram(name).rearrange("j (t p) -> (j t) p", p=P)
                        elif name == "rwkv_r_k":
                            src = k.ldram(name).rearrange("(t h) d -> t (h d)", h=2)
                        else:
                            src = k.ldram(name).rearrange("(t p) -> t p", p=P)
                        sp.dma_start(rows[at:at + n, t, :], src).then_inc(params_in, 16)
                        at += n
                sp.dma_start(shift_rows[:, :], k.ldram("state_rwkv_shift")).then_inc(states_in, 16)
                sp.dma_start(sconv_rows[:, :], k.ldram("state_ssm_conv").rearrange("b j c -> (b j) c")).then_inc(states_in, 16)
                sp.dma_start(fconv_rows[:, :], k.ldram("state_ffn_conv").rearrange("b j c -> (b j) c")).then_inc(states_in, 16)

            @block.scalar
            def _(act):
                for buf, name in ((k.dt_bias, "ssd_dt_bias"), (k.a_log, "ssd_a_log"), (k.ssd_d, "ssd_d"),
                                  (k.q_gain, "mla_q_norm_g"), (k.k_gain, "mla_k_norm_g")):
                    act.dma_start(buf[:, :], k.d[name][ds(k.layer, 1), :].to_broadcast([P, buf.shape[1]])).then_inc(small_in, 16)
                act.wait_ge(transposed, 1)
                for t, group in enumerate(PARAM_ROWS):
                    n = sum(x[1] for x in group)
                    nc.scalar.copy(k.params[:, t * P:t * P + n], banks[:, 0, t * P:t * P + n]).then_inc(copied, 1)
                act.wait_ge(transposed, 2)
                nc.scalar.copy(k.shift_T[:, :, :], banks[:, 1, 0:RT * NB]).then_inc(copied, 1)
                act.wait_ge(small_in, 80)

            @block.tensor
            def _(pe):
                pe.wait_ge(params_in, 16 * n_dma)
                for t, group in enumerate(PARAM_ROWS):
                    n = sum(x[1] for x in group)
                    last = nc.tensor.transpose(banks[:, 0, t * P:t * P + n], rows[0:n, t, :], k.col("ident", 0, n, n))
                last.then_inc(transposed, 1)
                pe.wait_ge(states_in, 48)
                for bank, src, n, w, t0 in ((1, shift_rows, RT, NB, 0), (2, sconv_rows, CT, 3 * NB, 0),
                                            (3, fconv_rows, FT, 2 * NB, 0), (4, fconv_rows, FT, 2 * NB, FT)):
                    for t in range(n):
                        last = nc.tensor.transpose(banks[:, bank, t * w:(t + 1) * w],
                                                   src[:, (t0 + t) * P:(t0 + t + 1) * P], k.col("ident", 0, w, w))
                    last.then_inc(transposed, 1)

            @block.vector
            def _(dve):
                dve.wait_ge(transposed, 3)
                nc.vector.tensor_copy(k.sconv_T[:, :, :], banks[:, 2, 0:CT * 24]).then_inc(copied, 1)
                dve.wait_ge(transposed, 4)
                nc.vector.tensor_copy(k.fconv_T[:, 0:FT, :], banks[:, 3, 0:FT * 16]).then_inc(copied, 1)
                dve.wait_ge(transposed, 5)
                nc.vector.tensor_copy(k.fconv_T[:, FT:2 * FT, :], banks[:, 4, 0:FT * 16]).then_inc(copied, 1)


def rms_norm(nc, k, src, gain, heads, rests):
    with Stage(nc) as st:
        sq = st.sb("norm_sq", [P, DT, T])
        inv = st.sb("norm_inv", [P, T])
        total = st.ps("norm_total", [P, BANK])
        squared, summed, inverse, scaled, rounded = (st.sem(n) for n in (
            "squared", "squares_summed", "inverse_root_ready", "norm_scaled", "norm_rounded"))
        with st.block() as block:
            @block.scalar
            def _(act):
                for d in range(DT):
                    nc.scalar.activation(sq[:, d, :], src[:, d, :], ACT.Square).then_inc(squared, 1)
                act.wait_ge(summed, 1)
                nc.scalar.activation(inv[:, :], total[:, 0:T], ACT.Ln, bias=k.col("eps"), scale=1.0 / D).then_inc(inverse, 1)
                act.wait_ge(inverse, 1)
                nc.scalar.activation(inv[:, :], inv[:, :], ACT.Exp, scale=-0.5).then_inc(inverse, 1)
                for d in range(DT):
                    act.wait_ge(scaled, d + 1)
                    nc.scalar.copy(heads[:, d, :], sq[:, d, :]).then_inc(rounded, 1)

            @block.tensor
            def _(pe):
                for d in range(DT):
                    pe.wait_ge(squared, d + 1)
                    last = nc.tensor.matmul(total[:, 0:T], k.col("ones"), sq[:, d, :], start=d == 0, stop=d == DT - 1)
                last.then_inc(summed, 1)

            @block.vector
            def _(dve):
                dve.wait_ge(inverse, 2)
                for d in range(DT):
                    nc.vector.scalar_tensor_tensor(sq[:, d, :], src[:, d, :], k.par(gain, d), inv[:, :],
                                                   ALU.mult, ALU.mult).then_inc(scaled, 1)
                for d in range(DT):
                    dve.wait_ge(rounded, d + 1)
                    nc.vector.tensor_tensor(rests[:, d, :], sq[:, d, :], heads[:, d, :].bitcast(F32), ALU.subtract)


def load_unit(sp, k, ring, loaded, split, w, first_col, width, turn, slot, first):
    if not first:
        sp.wait_ge(split, (turn - 1) * RING + slot + 1)
    at = (turn * RING + slot) * width + first_col
    sp.dma_start(ring[:, slot, :].rearrange("p (t n) -> p t n", n=width),
                 w[:, ds(at, width)].rearrange("(t p) n -> p t n", p=P)).then_inc(loaded[slot], 16)


def round_unit(nc, act, ring, heads, loaded, multiplied, rounded, turn, slot, first, per=16, base=0, tiles=DT * 2):
    act.wait_ge(loaded[slot], (turn + 1) * per)
    if not first:
        act.wait_ge(multiplied, (turn - 1) * RING + (slot + 1 + base))
    nc.scalar.copy(heads[:, slot, 0:tiles * P], ring[:, slot, 0:tiles * P]).then_inc(rounded, 1)


def rest_unit(nc, dve, ring, heads, rests, rounded, split, turn, slot, base=0, tiles=DT * 2):
    dve.wait_ge(rounded, turn * RING + (slot + 1 + base))
    nc.vector.tensor_tensor(rests[:, slot, 0:tiles * P], ring[:, slot, 0:tiles * P],
                            heads[:, slot, 0:tiles * P].bitcast(F32), ALU.subtract).then_inc(split, 1)


def product(nc, out, wh, wl, xh, xl, start, stop):
    nc.tensor.matmul(out, wh, xh, start=start, stop=False)
    nc.tensor.matmul(out, wh, xl, start=False, stop=False)
    return nc.tensor.matmul(out, wl, xh, start=False, stop=stop)


def following(turn, slot):
    return (turn, slot + 1, isinstance(turn, int) and turn == 0) if slot + 1 < RING else (turn + 1, 0, False)


def rwkv_project(nc, k):
    G, N = 2, RT // 2
    W = 1 + SEQ + NB * (NS + 1)
    w = k.ldram("w_in")
    with Stage(nc) as st:
        ring = st.sb("w_ring", [P, RING, DT * G * P])
        heads, rests = st.sb("w_heads", [P, RING, DT * G * P], F32R), st.sb("w_rests", [P, RING, DT * G * P], F32R)
        raw = st.sb("u_padded", [P, RING, G, W])
        diff = st.sb("shift_diff", [P, G, T])
        last_T = st.sb("last_u", [P, RT, 1 + NB])
        last_rows = st.sb("last_u_rows", [1 + NB, RWKV_IN])
        banks = st.ps("u_banks", [P, 8, BANK])
        loaded = [st.sem(f"weights_loaded{r}") for r in range(RING)]
        multiplied, evacuated, mixed = st.sem("unit_multiplied"), st.sem("unit_evacuated"), st.sem("unit_mixed")
        rounded, split = st.sem("weights_rounded"), st.sem("weights_split")
        padded, diffed, kept = st.sem("pads_zero"), st.sem("diff_ready"), st.sem("last_tokens_kept")
        turned, rows_out, stored = st.sem("last_transposed"), st.sem("last_rows_ready"), st.sem("last_stored")
        sample = raw[:, :, :, 1 + SEQ:W].rearrange("p r g (b s) -> p r g b s", s=NS + 1)
        with st.block() as block:
            @block.sync
            def _(sp):
                rounds(sp, N, RING, lambda i, r, first: load_unit(
                    sp, k, ring, loaded, split, w, OFF_RWKV, G * P, i, r, first))
                sp.wait_ge(rows_out, 7)
                sp.dma_start(k.ldram("p_rwkv_shift"), last_rows[0:1, :]).then_inc(stored, 16)
                sp.dma_start(k.ldram("s_rwkv_shift"), last_rows[1:1 + NB, :]).then_inc(stored, 16)
                sp.wait_ge(stored, 32)

            @block.tensor
            def _(pe):
                def unit(i, r, first):
                    pe.wait_ge(split, i * RING + (r + 1))
                    if not first:
                        pe.wait_ge(evacuated, (i - 1) * RING + r + 1)
                    for g in range(G):
                        for t in range(DT):
                            c = slice((t * G + g) * P, (t * G + g + 1) * P)
                            last = product(nc, banks[:, 2 * r + g, 0:T], heads[:, r, c], rests[:, r, c],
                                           k.hh[:, t, :], k.hl[:, t, :], t == 0, t == DT - 1)
                    last.then_inc(multiplied, 1)
                rounds(pe, N, RING, unit)
                pe.wait_ge(kept, 2 * N)
                for t in range(RT):
                    last = nc.tensor.transpose(banks[0:1 + NB, t // 4, t % 4 * P:(t % 4 + 1) * P], last_T[:, t, :], k.col("ident"))
                    if t % 4 == 3 or t == RT - 1:
                        last.then_inc(turned, 1)

            @block.scalar
            def _(act):
                round_unit(nc, act, ring, heads, loaded, multiplied, rounded, 0, 0, True)

                def unit(i, r, first):
                    if not (isinstance(i, int) and i * RING + r == N - 1):
                        round_unit(nc, act, ring, heads, loaded, multiplied, rounded, *following(i, r))
                    act.wait_ge(multiplied, i * RING + r + 1)
                    if not first:
                        act.wait_ge(mixed, (i - 1) * RING + r + 1)
                    nc.scalar.copy(raw[:, r, :, 1:1 + SEQ], banks[:, 2 * r:2 * r + 2, 0:SEQ])
                    nc.scalar.copy(sample[:, r, :, :, 1:NS + 1],
                                   banks[:, 2 * r:2 * r + 2, SEQ:T].rearrange("p g (b s) -> p g b s", s=NS)).then_inc(evacuated, 1)
                rounds(act, N, RING, unit)
                for q in range(7):
                    act.wait_ge(turned, q + 1)
                    n = min(4, RT - 4 * q) * P
                    nc.scalar.copy(last_rows[:, q * 512:q * 512 + n], banks[0:1 + NB, q, 0:n]).then_inc(rows_out, 1)

            @block.vector
            def _(dve):
                nc.vector.memset(raw[:, :, :, 0:1], 0.0).then_inc(padded, 1)
                dve.wait_ge(padded, 1)
                rest_unit(nc, dve, ring, heads, rests, rounded, split, 0, 0)

                def unit(i, r, first):
                    u = i * RING + r
                    if not (isinstance(i, int) and u == N - 1):
                        rest_unit(nc, dve, ring, heads, rests, rounded, split, *following(i, r)[0:2])
                    dve.wait_ge(evacuated, u + 1)
                    if not (first and r == 0):
                        dve.wait_ge(mixed, u)
                    nc.vector.tensor_copy(sample[:, r, :, :, 0], k.shift_T[:, ds(u * G, G), :]).then_inc(diffed, 1)
                    nc.vector.tensor_tensor(diff[:, :, 0:SEQ], raw[:, r, :, 0:SEQ], raw[:, r, :, 1:SEQ + 1], ALU.subtract)
                    nc.vector.tensor_copy(last_T[:, ds(u * G, G), 0:1], raw[:, r, :, SEQ:SEQ + 1]).then_inc(kept, 1)
                    nc.vector.tensor_copy(last_T[:, ds(u * G, G), 1:1 + NB], sample[:, r, :, :, NS]).then_inc(kept, 1)
                    dve.wait_ge(diffed, u * 2 + 1)
                    nc.vector.tensor_tensor(diff[:, :, SEQ:T].rearrange("p g (b s) -> p g b s", s=NS),
                                            sample[:, r, :, :, 0:NS], sample[:, r, :, :, 1:NS + 1],
                                            ALU.subtract).then_inc(diffed, 1)
                    dve.wait_ge(diffed, u * 2 + 2)
                    for g in range(G):
                        mu = k.params[:, ds(u * G + (PCOL["rwkv_shift_mu"][0] + g), 1)]
                        nc.vector.scalar_tensor_tensor(k.fT[:, ds(u * G + g, 1), 0:SEQ].rearrange("p o t -> p (o t)"), diff[:, g, 0:SEQ], mu,
                                                       raw[:, r, g, 1:SEQ + 1], ALU.mult, ALU.add)
                        last = nc.vector.scalar_tensor_tensor(
                            k.fT[:, ds(u * G + g, 1), SEQ:T].rearrange("p o (b s) -> p (o b) s", s=NS),
                            diff[:, g, SEQ:T].rearrange("p (b s) -> p b s", s=NS), mu,
                            sample[:, r, g, :, 1:NS + 1], ALU.mult, ALU.add)
                    last.then_inc(mixed, 1)
                rounds(dve, N, RING, unit)


def rwkv_prepare(nc, k):
    r_f, k_f, v_f = k.fT[:, 0:8, :], k.fT[:, 8:16, :], k.fT[:, 16:24, :]
    with Stage(nc) as st:
        wa_up = st.sb("wa_up", [P, D])
        g_up = st.sb("g_up", [P, D])
        lo = st.sb("tanh_w_lo", [P, T])
        aT = st.sb("aT", [P, DT, T])
        lw = st.sb("log_decay", [P, DT, T])
        cum = st.sb("log_decay_sum", [P, DT, SEQ])
        kk = st.sb("kk", [P, DT, T])
        tmp = st.sb("rwkv_tmp", [P, DT, T])
        banks = st.ps("prep_banks", [P, 8, BANK])
        up_in = st.sem("lora_weights_loaded")
        lo_ready = st.sem("lora_inputs_ready")
        w_made, a_made, g_made = st.sem("w_product"), st.sem("a_product"), st.sem("g_product")
        w_sig, a_sig, g_kept = st.sem("w_sigmoid"), st.sem("a_sigmoid"), st.sem("g_kept")
        step = st.sem("dve_step")
        kk_sq, kk_sum, kk_cut = st.sem("kk_squared"), st.sem("kk_summed"), st.sem("kk_sum_clamped")
        kk_raw, kk_root = st.sem("kk_raw_ready"), st.sem("kk_root_ready")
        bonus_in, bonus_sum, bonus_out = st.sem("bonus_products"), st.sem("bonus_summed"), st.sem("bonus_ready")
        exp_arg, exp_out, exp_used = st.sem("exp_argument_ready"), st.sem("exp_ready"), st.sem("exp_used")
        packed = st.sem("sample_packed")
        with st.block() as block:
            @block.sync
            def _(sp):
                sp.dma_start(wa_up[0:64, :], k.ldram("rwkv_w_up")).then_inc(up_in, 16)
                sp.dma_start(wa_up[64:128, :], k.ldram("rwkv_a_up")).then_inc(up_in, 16)
                sp.dma_start(g_up[:, :], k.ldram("rwkv_g_up")).then_inc(up_in, 16)

            @block.tensor
            def _(pe):
                pe.wait_ge(up_in, 48)
                pe.wait_ge(lo_ready, 2)
                for d in range(DT):
                    cols = slice(d * P, (d + 1) * P)
                    if d >= 2:
                        pe.wait_ge(w_sig, d - 1)
                        pe.wait_ge(a_sig, d - 1)
                        pe.wait_ge(g_kept, d - 1)
                    nc.tensor.matmul(banks[:, d % 2, 0:T], wa_up[0:64, cols], lo[0:64, :], start=True, stop=True).then_inc(w_made, 1)
                    nc.tensor.matmul(banks[:, 2 + d % 2, 0:T], wa_up[64:128, cols], k.fT[64:128, 24, :], start=True, stop=True).then_inc(a_made, 1)
                    nc.tensor.matmul(banks[:, 4 + d % 2, 0:T], g_up[:, cols], k.fT[:, 25, :], start=True, stop=True).then_inc(g_made, 1)
                pe.wait_ge(kk_sq, 1)
                for d in range(DT):
                    if d >= 2:
                        pe.wait_ge(kk_cut, d - 1)
                    nc.tensor.matmul(banks[:, 6 + d % 2, 0:T], k.col("block64"), tmp[:, d, :], start=True, stop=True).then_inc(kk_sum, 1)
                pe.wait_ge(bonus_in, 1)
                pe.wait_ge(kk_cut, DT)
                for d in range(DT):
                    if d >= 2:
                        pe.wait_ge(bonus_out, d - 1)
                    nc.tensor.matmul(banks[:, 6 + d % 2, 0:T], k.col("block64"), tmp[:, d, :], start=True, stop=True).then_inc(bonus_sum, 1)

            @block.scalar
            def _(act):
                nc.scalar.activation(lo[0:64, :], k.fT[0:64, 24, :], ACT.Tanh).then_inc(lo_ready, 1)
                nc.scalar.activation(k.fT[:, 25, :], k.fT[:, 25, :], ACT.Sigmoid).then_inc(lo_ready, 1)
                for d in range(DT):
                    act.wait_ge(w_made, d + 1)
                    nc.scalar.activation(lw[:, d, :], banks[:, d % 2, 0:T], ACT.Sigmoid, bias=k.par("rwkv_w0", d)).then_inc(w_sig, 1)
                    act.wait_ge(a_made, d + 1)
                    nc.scalar.activation(aT[:, d, :], banks[:, 2 + d % 2, 0:T], ACT.Sigmoid, bias=k.par("rwkv_a0", d)).then_inc(a_sig, 1)
                act.wait_ge(kk_raw, 1)
                nc.scalar.activation(tmp[:, :, :], kk[:, :, :], ACT.Square).then_inc(kk_sq, 1)
                act.wait_ge(kk_cut, DT)
                nc.scalar.activation(tmp[:, :, :], tmp[:, :, :], ACT.Sqrt).then_inc(kk_root, 1)
                act.wait_ge(exp_arg, 1)
                nc.scalar.activation(k.samT[:, 1, :, :], lw[:, :, SEQ:T], ACT.Exp).then_inc(exp_out, 1)
                act.wait_ge(bonus_out, DT)
                nc.scalar.activation(tmp[:, :, 0:SEQ], cum[:, :, :], ACT.Exp).then_inc(exp_out, 1)
                for n in range(2):
                    act.wait_ge(exp_arg, n + 2)
                    nc.scalar.activation(tmp[:, :, 0:SEQ], tmp[:, :, 0:SEQ], ACT.Exp).then_inc(exp_out, 1)
                act.wait_ge(exp_used, 4)
                nc.scalar.activation(tmp[:, :, 0:SEQ], cum[:, :, :], ACT.Exp, scale=-1.0).then_inc(exp_out, 1)

            @block.vector
            def _(dve):
                def par(name):
                    return bc(k.par(name, 0, DT), T)
                c = Chain(dve, step)
                for d in range(DT):
                    dve.wait_ge(g_made, d + 1)
                    nc.vector.tensor_copy(k.gT[:, d, :], banks[:, 4 + d % 2, 0:SEQ])
                    nc.vector.tensor_copy(k.sam_gate[:, d, :], banks[:, 4 + d % 2, SEQ:T]).then_inc(g_kept, 1)
                nc.vector.tensor_tensor(kk[:, :, :], k_f, par("rwkv_k_k"), ALU.mult).then_inc(kk_raw, 1)
                dve.wait_ge(a_sig, DT)
                c(nc.vector.scalar_tensor_tensor(cum[:, :, :],
                                                 aT[:, :, 0:SEQ], -1.0, bc(k.par("rwkv_k_a", 0, DT), SEQ), ALU.add, ALU.mult))
                c(nc.vector.scalar_tensor_tensor(k_f[:, :, 0:SEQ], cum[:, :, :], 1.0, k_f[:, :, 0:SEQ], ALU.add, ALU.mult))
                c(nc.vector.scalar_tensor_tensor(cum[:, :, 0:NSAM], aT[:, :, SEQ:T], -1.0, bc(k.par("rwkv_k_a", 0, DT), NSAM), ALU.add, ALU.mult))
                c(nc.vector.scalar_tensor_tensor(k_f[:, :, SEQ:T], cum[:, :, 0:NSAM], 1.0, k_f[:, :, SEQ:T], ALU.add, ALU.mult))
                dve.wait_ge(kk_sq, 1)
                for d in range(DT):
                    dve.wait_ge(kk_sum, d + 1)
                    nc.vector.tensor_scalar(tmp[:, d, :], banks[:, 6 + d % 2, 0:T], 1e-24, None, ALU.max).then_inc(kk_cut, 1)
                dve.wait_ge(w_sig, DT)
                c(nc.vector.tensor_scalar(lw[:, :, :], lw[:, :, :], -0.6065306597126334, None, ALU.mult))
                for d in range(DT):
                    last = nc.vector.tensor_tensor_scan(cum[:, d, :], k.col("keep"), lw[:, d, 0:SEQ], 0.0, ALU.mult, ALU.add)
                c(last)
                dve.wait_ge(kk_root, 1)
                c(nc.vector.reciprocal(tmp[:, :, :], tmp[:, :, :]))
                c(nc.vector.tensor_tensor(kk[:, :, :], kk[:, :, :], tmp[:, :, :], ALU.mult))
                c(nc.vector.tensor_tensor(tmp[:, :, :], r_f, k_f, ALU.mult))
                nc.vector.tensor_tensor(tmp[:, :, :], tmp[:, :, :], par("rwkv_r_k"), ALU.mult).then_inc(bonus_in, 1)
                c(nc.vector.tensor_tensor(aT[:, :, :], aT[:, :, :], kk[:, :, :], ALU.mult))
                for d in range(DT):
                    dve.wait_ge(bonus_sum, d + 1)
                    nc.vector.tensor_tensor(k.bonusT[:, d, :], banks[:, 6 + d % 2, 0:SEQ], v_f[:, d, 0:SEQ], ALU.mult)
                    nc.vector.tensor_tensor(k.sam_bonus[:, d, :], banks[:, 6 + d % 2, SEQ:T], v_f[:, d, SEQ:T], ALU.mult).then_inc(bonus_out, 1)
                for n, src in ((0, r_f), (2, k_f), (3, v_f), (4, kk), (5, aT)):
                    nc.vector.tensor_copy(k.samT[:, n, :, :], src[:, :, SEQ:T]).then_inc(packed, 1)
                dve.wait_ge(packed, 5)
                nc.vector.tensor_copy(k.chunk_decay[:, :, :], cum[:, :, :].rearrange("p d (c n) -> p d c n", n=CH)[:, :, :, CH - 1]).then_inc(exp_arg, 1)
                dve.wait_ge(exp_out, 2)
                nc.vector.tensor_tensor(r_f[:, :, 0:SEQ], r_f[:, :, 0:SEQ], tmp[:, :, 0:SEQ], ALU.mult).then_inc(exp_used, 1)
                dve.wait_ge(exp_used, 1)
                nc.vector.tensor_tensor(tmp[:, :, 0:SEQ], cum[:, :, :], lw[:, :, 0:SEQ], ALU.subtract).then_inc(exp_arg, 1)
                dve.wait_ge(exp_out, 3)
                nc.vector.scalar_tensor_tensor(k.alphaT[:, :, :], kk[:, :, 0:SEQ], -1.0, tmp[:, :, 0:SEQ], ALU.mult, ALU.mult).then_inc(exp_used, 1)
                dve.wait_ge(exp_used, 2)
                nc.vector.tensor_tensor(tmp[:, :, 0:SEQ].rearrange("p d (c n) -> p d c n", n=CH), bc(k.chunk_decay[:, :, :], CH),
                                        cum[:, :, :].rearrange("p d (c n) -> p d c n", n=CH), ALU.subtract).then_inc(exp_arg, 1)
                dve.wait_ge(exp_out, 4)
                nc.vector.tensor_tensor(k.bendT[:, :, :], aT[:, :, 0:SEQ], tmp[:, :, 0:SEQ], ALU.mult).then_inc(exp_used, 1)
                nc.vector.tensor_tensor(k.kendT[:, :, :], k_f[:, :, 0:SEQ], tmp[:, :, 0:SEQ], ALU.mult).then_inc(exp_used, 1)
                dve.wait_ge(exp_out, 5)
                nc.vector.tensor_tensor(k.betaT[:, :, :], aT[:, :, 0:SEQ], tmp[:, :, 0:SEQ], ALU.mult).then_inc(exp_used, 1)
                nc.vector.tensor_tensor(k_f[:, :, 0:SEQ], k_f[:, :, 0:SEQ], tmp[:, :, 0:SEQ], ALU.mult).then_inc(exp_used, 1)
        with st.block() as block:
            @block.scalar
            def _(act):
                nc.scalar.activation(k.chunk_decay[:, :, :], k.chunk_decay[:, :, :], ACT.Exp)


def rwkv_tile(nc, k, tile):
    c0 = tile * P
    with Stage(nc) as st:
        L = st.sb("L", [P, 4, 4, P])
        Ln = st.sb("L_level", [P, 4, 4, P])
        X = st.sb("X", [P, 4, 4, P])
        Y = st.sb("Y", [P, 4, 4, P])
        BR = st.sb("BR", [P, 4, 4, P])
        KR = st.sb("KR", [P, 4, 4, P])
        Z = st.sb("Z", [P, 4, 4, P])
        v_tm = st.sb("v_tm", [P, D])
        rhs = st.sb("sa_rhs", [P, D])
        y = L[:, 2:4, :, :].rearrange("p a b c -> p (a b c)")
        stat, stat2 = st.sb("head_mean", [P, 16]), st.sb("head_var", [P, 16])
        KA = Z
        sa = Ln[:, 0:2, :, :].rearrange("p a b c -> p (a b c)")
        state_rows = Z[:, 0, :, :].rearrange("p a b -> p (a b)").rearrange("p (t n) -> p t n", n=64)
        bend_tm = X[:, 0:2, :, :].rearrange("p a b c -> p (a b c)")
        kend_tm = X[:, 2:4, :, :].rearrange("p a b c -> p (a b c)")
        sq = L[:, 0:2, :, :].rearrange("p a b c -> p (a b c)")
        banks = st.ps("tile_banks", [P, 8, BANK])
        S = k.Sbd
        made, kept = st.sem("pair_products_made"), st.sem("pair_products_kept")
        kav_made, kav_kept = st.sem("kav_made"), st.sem("kav_kept")
        v_turned, v_kept = st.sem("v_transposed"), st.sem("v_kept")
        level_in = st.sem("level_masked")
        z_made, z_kept = st.sem("z_made"), st.sem("z_kept")
        xy_made, x_kept, y_kept = st.sem("xy_made"), st.sem("x_kept"), st.sem("y_kept")
        e_turned, e_kept = st.sem("ends_transposed"), st.sem("ends_kept")
        as_made, rhs_kept, rs_kept = st.sem("state_products_made"), st.sem("rhs_ready"), st.sem("rho_state_kept")
        sa_made, sa_kept = st.sem("sa_made"), st.sem("sa_kept")
        s_made, s_kept = st.sem("state_update_made"), st.sem("state_kept")
        y_made, y_sum = st.sem("y_made"), st.sem("y_summed")
        step = st.sem("dve_step")
        sq_ready, inv_ready, normed = st.sem("squares_ready"), st.sem("inverse_root"), st.sem("y_normed")
        o_turned, o_kept = st.sem("y_transposed"), st.sem("y_T_ready")
        st_turned, st_kept, st_out = st.sem("state_turned"), st.sem("state_rows_ready"), st.sem("state_stored")

        def head_of(q, i):
            return 4 * (q % 2) + i, 64 * (q // 2)

        def nat(buf, q, i):
            t, p0 = head_of(q, i)
            return buf[:, t * P + p0:t * P + p0 + 64]

        with st.block() as block:
            @block.tensor
            def _(pe):
                for t in range(DT):
                    last = nc.tensor.transpose(banks[:, 6 + t // 4, t % 4 * P:(t % 4 + 1) * P],
                                               k.fT[:, 16 + t, c0:c0 + P], k.col("ident"))
                last.then_inc(v_turned, 1)
                kap, rho = k.fT[:, 8:16, :], k.fT[:, 0:8, :]
                cols = slice(c0, c0 + P)
                for q in range(4):
                    if q:
                        pe.wait_ge(kept, 4 * q)
                    for n, (a, b) in enumerate(((k.alphaT, k.betaT), (kap, k.alphaT), (k.betaT, rho), (kap, rho))):
                        for i in range(4):
                            t, p0 = head_of(q, i)
                            last = nc.tensor.matmul(banks[:, n, i * P:(i + 1) * P], a[p0:p0 + 64, t, cols],
                                                    b[p0:p0 + 64, t, cols], start=True, stop=True, skip_group_check=True)
                        last.then_inc(made, 1)
                pe.wait_ge(kept, 16)
                pe.wait_ge(v_kept, 2)
                for half in range(2):
                    for h in range(8 * half, 8 * half + 8):
                        t, par = h // 2, h % 2
                        q, i = 2 * par + t // 4, t % 4
                        last = nc.tensor.matmul(banks[:, 4 + half, h % 8 * 64:(h % 8 + 1) * 64], KA[:, q, i, :],
                                                v_tm[:, h * 64:(h + 1) * 64], start=True, stop=True, skip_group_check=True)
                    last.then_inc(kav_made, 1)
                for q in range(4):
                    pe.wait_ge(level_in, q + 1)
                    for i in range(4):
                        last = nc.tensor.transpose(banks[:, q, i * P:(i + 1) * P], Ln[:, q, i, :], k.col("ident"))
                    last.then_inc(z_made, 1)
                for n in range(1, 6):
                    for q in range(4):
                        pe.wait_ge(level_in, 4 * n + q + 1)
                        pe.wait_ge(y_kept, 4 * (n - 1) + q + 1)
                        for i in range(4):
                            last = nc.tensor.matmul(banks[:, q, i * P:(i + 1) * P], Ln[:, q, i, :], Y[:, q, i, :],
                                                    start=True, stop=True, skip_group_check=True)
                        last.then_inc(z_made, 1)
                    for q in range(4):
                        pe.wait_ge(z_kept, 4 * (n - 1) + q + 1)
                        pe.wait_ge(x_kept, 4 * (n - 1) + q + 1)
                        if n == 1 and q == 0:
                            pe.wait_ge(kav_kept, 2)
                        if q >= 2 or n > 1:
                            m = 4 * n + q - 2
                            pe.wait_ge(y_kept, m + 1)
                            pe.wait_ge(x_kept, min(m + 1, 20))
                        b = 4 + 2 * (q % 2)
                        for i in range(4):
                            last = nc.tensor.matmul(banks[:, b, i * P:(i + 1) * P], X[:, q, i, :], Z[:, q, i, :],
                                                    start=True, stop=True, skip_group_check=True)
                        if n < 5:
                            for i in range(4):
                                last = nc.tensor.matmul(banks[:, b + 1, i * P:(i + 1) * P], Z[:, q, i, :], X[:, q, i, :],
                                                        start=True, stop=True, skip_group_check=True)
                        last.then_inc(xy_made, 1)
                for n, src in enumerate((k.bendT, k.kendT)):
                    for t in range(DT):
                        last = nc.tensor.transpose(banks[:, 2 * n + t // 4, t % 4 * P:(t % 4 + 1) * P],
                                                   src[:, t, c0:c0 + P], k.col("ident"))
                    last.then_inc(e_turned, 1)
                pe.wait_ge(y_kept, 24)
                pe.wait_ge(e_kept, 2)
                for c in range(2):
                    if c:
                        pe.wait_ge(s_kept, 1)
                        pe.wait_ge(rs_kept, 1)
                    for n, src in enumerate((k.alphaT, rho)):
                        for t in range(DT):
                            last = nc.tensor.matmul(banks[:, 4 * n + t // 4, t % 4 * P:(t % 4 + 1) * P], src[:, t, cols],
                                                    S[:, t, :], start=True, stop=True, skip_group_check=True)
                        last.then_inc(as_made, 1)
                    pe.wait_ge(rhs_kept, c + 1)
                    for h in range(16):
                        t, par = h // 2, h % 2
                        last = nc.tensor.matmul(banks[:, 2 + h // 8, h % 8 * 64:(h % 8 + 1) * 64], Y[:, 2 * par + t // 4, t % 4, :],
                                                rhs[:, h * 64:(h + 1) * 64], start=True, stop=True, skip_group_check=True)
                    last.then_inc(sa_made, 1)
                    pe.wait_ge(sa_kept, c + 1)
                    rows = slice(64 * c, 64 * c + 64)
                    for t in range(DT):
                        w = slice(t * P, (t + 1) * P)
                        out = banks[:, 6 + t // 4, t % 4 * P:(t % 4 + 1) * P]
                        nc.tensor.matmul(out, bend_tm[rows, w], sa[rows, w], start=True, stop=False, skip_group_check=True)
                        last = nc.tensor.matmul(out, kend_tm[rows, w], v_tm[rows, w], start=False, stop=True, skip_group_check=True)
                    last.then_inc(s_made, 1)
                for h in range(16):
                    t, par = h // 2, h % 2
                    q, i = 2 * par + t // 4, t % 4
                    out = banks[:, 2 + h // 8, h % 8 * 64:(h % 8 + 1) * 64]
                    w = slice(h * 64, (h + 1) * 64)
                    nc.tensor.matmul(out, BR[:, q, i, :], sa[:, w], start=True, stop=False, skip_group_check=True)
                    last = nc.tensor.matmul(out, KR[:, q, i, :], v_tm[:, w], start=False, stop=True, skip_group_check=True)
                last.then_inc(y_made, 1)
                if tile == 1:
                    pe.wait_ge(s_kept, 2)
                    for t in range(DT):
                        last = nc.tensor.transpose(banks[:, 6 + t // 4, t % 4 * P:(t % 4 + 1) * P], S[:, t, :], k.col("ident"))
                    last.then_inc(st_turned, 1)
                pe.wait_ge(normed, 1)
                for t in range(DT):
                    last = nc.tensor.transpose(banks[:, 4 + t // 4, t % 4 * P:(t % 4 + 1) * P], y[:, t * P:(t + 1) * P], k.col("ident"))
                last.then_inc(o_turned, 1)

            @block.scalar
            def _(act):
                act.wait_ge(v_turned, 1)
                for half in range(2):
                    nc.scalar.copy(v_tm[:, half * 512:(half + 1) * 512], banks[:, 6 + half, :]).then_inc(v_kept, 1)
                for half in range(2):
                    act.wait_ge(kav_made, half + 1)
                    nc.scalar.copy(rhs[:, half * 512:(half + 1) * 512], banks[:, 4 + half, :]).then_inc(kav_kept, 1)
                for n in range(1, 6):
                    for q in range(4):
                        act.wait_ge(z_made, 4 * n + q + 1)
                        if n > 1:
                            act.wait_ge(xy_made, 4 * (n - 2) + q + 1)
                        nc.scalar.copy(Z[:, q, :, :], banks[:, q, :]).then_inc(z_kept, 1)
                act.wait_ge(xy_made, 20)
                for n, dst in enumerate((bend_tm, kend_tm)):
                    act.wait_ge(e_turned, n + 1)
                    nc.scalar.copy(dst, banks[:, 2 * n:2 * n + 2, :]).then_inc(e_kept, 1)
                for c in range(2):
                    rows = slice(64 * c, 64 * c + 64)
                    act.wait_ge(as_made, 2 * c + 2)
                    nc.scalar.copy(y[rows, :], banks[rows, 4:6, :]).then_inc(rs_kept, 1)
                    act.wait_ge(sa_made, c + 1)
                    nc.scalar.copy(sa[rows, :], banks[rows, 2:4, :]).then_inc(sa_kept, 1)
                act.wait_ge(y_sum, 1)
                nc.scalar.activation(sq, y, ACT.Square).then_inc(sq_ready, 1)
                act.wait_ge(y_sum, 2)
                nc.scalar.activation(stat2[:, :], stat2[:, :], ACT.Ln, bias=k.col("rwkv_eps"), scale=1.0 / 64).then_inc(inv_ready, 1)
                act.wait_ge(inv_ready, 1)
                nc.scalar.activation(stat2[:, :], stat2[:, :], ACT.Exp, scale=-0.5).then_inc(inv_ready, 1)
                if tile == 1:
                    act.wait_ge(st_turned, 1)
                    nc.scalar.copy(state_rows[0:64, :, :], banks[0:64, 6:8, :].rearrange("p a (t n) -> p (a t) n", n=P)[:, :, 0:64]).then_inc(st_kept, 1)
                    nc.scalar.copy(state_rows[64:128, :, :], banks[64:128, 6:8, :].rearrange("p a (t n) -> p (a t) n", n=P)[:, :, 64:128]).then_inc(st_kept, 1)

            @block.gpsimd
            def _(pool):
                for n in range(6):
                    for q in range(4):
                        if n == 0:
                            pool.wait_ge(kept, 4 * q + 1)
                        else:
                            pool.wait_ge(z_made, 4 * (n - 1) + q + 1)
                            if n == 1:
                                pool.wait_ge(x_kept, q + 1)
                        nc.gpsimd.tensor_tensor(Ln[:, q, :, :], L[:, q, :, :], k.col(f"level{n}").unsqueeze(1).to_broadcast([P, 4, P]),
                                                ALU.mult).then_inc(level_in, 1)

            @block.vector
            def _(dve):
                def m(name):
                    return k.col(name).unsqueeze(1).to_broadcast([P, 4, P])

                def bank(b):
                    return banks[:, b, :].rearrange("p (i t) -> p i t", t=P)
                for q in range(4):
                    for n, (dst, mask) in enumerate(((L, None), (KA, "cmask_lt"), (BR, "cmask_le"), (KR, "cmask_le"))):
                        dve.wait_ge(made, 4 * q + n + 1)
                        if mask is None:
                            nc.vector.tensor_copy(dst[:, q, :, :], bank(n)).then_inc(kept, 1)
                        else:
                            nc.vector.tensor_tensor(dst[:, q, :, :], bank(n), m(mask), ALU.mult).then_inc(kept, 1)
                for q in range(4):
                    dve.wait_ge(level_in, q + 1)
                    nc.vector.tensor_tensor(X[:, q, :, :], Ln[:, q, :, :], m("ident"), ALU.add).then_inc(x_kept, 1)
                    dve.wait_ge(z_made, q + 1)
                    nc.vector.tensor_tensor(Y[:, q, :, :], bank(q), m("ident"), ALU.add).then_inc(y_kept, 1)
                for n in range(1, 6):
                    for q in range(4):
                        dve.wait_ge(xy_made, 4 * (n - 1) + q + 1)
                        b = 4 + 2 * (q % 2)
                        dve.wait_ge(y_kept, 4 * (n - 1) + q + 1)
                        nc.vector.tensor_tensor(Y[:, q, :, :], bank(b), Y[:, q, :, :], ALU.add).then_inc(y_kept, 1)
                        if n < 5:
                            dve.wait_ge(x_kept, 4 * (n - 1) + q + 1)
                            nc.vector.tensor_tensor(X[:, q, :, :], bank(b + 1), X[:, q, :, :], ALU.add).then_inc(x_kept, 1)
                c_ = Chain(dve, step)
                for c in range(2):
                    rows = slice(64 * c, 64 * c + 64)
                    dve.wait_ge(as_made, 2 * c + 1)
                    if c == 0:
                        dve.wait_ge(kav_kept, 2)
                    nc.vector.tensor_tensor(rhs[rows, :].rearrange("p (a n) -> p a n", a=2), banks[rows, 0:2, :],
                                            rhs[rows, :].rearrange("p (a n) -> p a n", a=2), ALU.add).then_inc(rhs_kept, 1)
                    dve.wait_ge(as_made, 2 * c + 2)
                    chunk = 2 * tile + c
                    c_(nc.vector.tensor_tensor(S[:, :, :], S[:, :, :], k.chunk_decay[:, :, chunk:chunk + 1].to_broadcast([P, DT, P]), ALU.mult))
                    dve.wait_ge(s_made, c + 1)
                    upd = banks[:, 6:8, :].rearrange("p a (t n) -> p (a t) n", n=P)
                    nc.vector.tensor_tensor(S[0:64, :, 0:64], upd[0:64, :, 0:64], S[0:64, :, 0:64], ALU.add)
                    nc.vector.tensor_tensor(S[64:128, :, 64:128], upd[64:128, :, 64:128], S[64:128, :, 64:128], ALU.add).then_inc(s_kept, 1)
                dve.wait_ge(y_made, 1)
                dve.wait_ge(rs_kept, 2)
                yh = y.rearrange("p (h v) -> p h v", v=64)
                c_(nc.vector.tensor_tensor(y.rearrange("p (a n) -> p a n", a=2), banks[:, 2:4, :],
                                           y.rearrange("p (a n) -> p a n", a=2), ALU.add))
                c_(nc.vector.tensor_reduce(stat[:, :], yh, AX.X, ALU.add))
                c_(nc.vector.tensor_scalar(stat[:, :], stat[:, :], 1.0 / 64, None, ALU.mult))
                nc.vector.tensor_tensor(yh, yh, bc(stat[:, :], 64), ALU.subtract).then_inc(y_sum, 1)
                dve.wait_ge(sq_ready, 1)
                nc.vector.tensor_reduce(stat2[:, :], sq.rearrange("p (h v) -> p h v", v=64), AX.X, ALU.add).then_inc(y_sum, 1)
                dve.wait_ge(inv_ready, 2)
                nc.vector.tensor_tensor(yh, yh, bc(stat2[:, :], 64), ALU.mult).then_inc(normed, 1)
                dve.wait_ge(o_turned, 1)
                cols = slice(c0, c0 + P)
                for t in range(DT):
                    last = nc.vector.tensor_scalar(k.o_rwkv[:, t, cols], banks[:, 4 + t // 4, t % 4 * P:(t % 4 + 1) * P],
                                                   k.par("rwkv_ln_g", t), k.par("rwkv_ln_b", t), ALU.mult, ALU.add)
                c_(last)
                c_(nc.vector.tensor_tensor(k.o_rwkv[:, :, cols], k.o_rwkv[:, :, cols], k.bonusT[:, :, cols], ALU.add))
                c_(nc.vector.tensor_tensor(k.o_rwkv[:, :, cols], k.o_rwkv[:, :, cols], k.gT[:, :, cols], ALU.mult))

            if tile == 1:
                @block.sync
                def _(sp):
                    sp.wait_ge(st_kept, 2)
                    sp.dma_start(k.ldram("p_rwkv").rearrange("o (t h) v k -> (o h v) t k", h=2), state_rows[:, :, :]).then_inc(st_out, 16)
                    sp.wait_ge(st_out, 16)


def mla_project(nc, k):
    w = k.ldram("w_in")
    with Stage(nc) as st:
        ring = st.sb("mla_w", [P, 4, DT, 256])
        heads, rests = st.sb("mla_w_heads", [P, 2, DT, 256], F32R), st.sb("mla_w_rests", [P, 2, DT, 256], F32R)
        sq = st.sb("mla_sq", [P, 6, T])
        inv = st.sb("mla_inv", [P, 2, T])
        kpeT = st.sb("kpe_raw_T", [ROPE, T])
        lat_tm = st.sb("latent_tm", [P, 3, KVRANK])
        rot = st.sb("kpe_products", [P, 3, 4, 32])
        banks = st.ps("mla_banks", [P, 8, BANK])
        loaded = [st.sem(f"weights_loaded{i}") for i in range(4)]
        rounded, split = st.sem("weights_rounded"), st.sem("weights_split")
        made, kept, squared = st.sem("products_made"), st.sem("products_kept"), st.sem("squared")
        summed, inverse, scaled = st.sem("summed"), st.sem("inverse_root"), st.sem("scaled")
        turned, lat_kept, step = st.sem("transposed"), st.sem("latent_rows_ready"), st.sem("dve_step")
        rotated, back, back_kept, stored = st.sem("rotated"), st.sem("kpe_turned_back"), st.sem("kpe_T_ready"), st.sem("stored")
        with st.block() as block:
            @block.sync
            def _(sp):
                for i in range(3):
                    sp.dma_start(ring[:, i, :, :], w[:, OFF_MLA + 256 * i:OFF_MLA + 256 * (i + 1)].rearrange("(t p) n -> p t n", p=P)).then_inc(loaded[i], 16)
                for j in range(2):
                    sp.dma_start(ring[:, 3, :, j * ROPE:(j + 1) * ROPE], w[:, OFF_MLA + 768:OFF_MLA + 832].rearrange("(t p) n -> p t n", p=P)).then_inc(loaded[3], 16)
                sp.wait_ge(lat_kept, 2)
                sp.dma_start(k.ldram("p_kv_latent").rearrange("o (n p) r -> p (o n) r", p=P), lat_tm[:, 0:2, :]).then_inc(stored, 16)
                sp.dma_start(k.ldram("s_kv_latent").rearrange("b t r -> (b t) r"), lat_tm[0:NSAM, 2, :]).then_inc(stored, 16)
                sp.wait_ge(rotated, 3)
                sp.dma_start(k.ldram("p_k_rope").rearrange("o (n p) r -> p (o n) r", p=P), k.kpe_tm[:, 0:2, :]).then_inc(stored, 16)
                sp.dma_start(k.ldram("s_k_rope").rearrange("b t r -> (b t) r"), k.kpe_tm[0:NSAM, 2, :]).then_inc(stored, 16)
                sp.wait_ge(stored, 64)

            @block.tensor
            def _(pe):
                for i in range(3):
                    pe.wait_ge(split, i + 1)
                    for g in range(2):
                        for t in range(DT):
                            c = slice(g * P, (g + 1) * P)
                            last = product(nc, banks[:, 2 * i + g, 0:T], heads[:, i % 2, t, c], rests[:, i % 2, t, c],
                                           k.hh[:, t, :], k.hl[:, t, :], t == 0, t == DT - 1)
                        last.then_inc(made, 1)
                pe.wait_ge(split, 4)
                for t in range(DT):
                    last = product(nc, banks[:, 6, 0:T], heads[:, 1, t, 0:P], rests[:, 1, t, 0:P],
                                   k.hh[:, t, :], k.hl[:, t, :], t == 0, t == DT - 1)
                last.then_inc(made, 1)
                pe.wait_ge(squared, 6)
                for n, (t0, t1) in enumerate(((0, 4), (4, 6))):
                    for t in range(t0, t1):
                        last = nc.tensor.matmul(banks[:, n, 0:T], k.col("ones"), sq[:, t, :], start=t == t0, stop=t == t1 - 1)
                    last.then_inc(summed, 1)
                pe.wait_ge(kept, 7)
                for n, (first, rows) in enumerate(TOK):
                    last = nc.tensor.transpose(banks[0:rows, 2, n * ROPE:(n + 1) * ROPE], kpeT[:, first:first + rows], k.col("ident", 0, ROPE, ROPE))
                last.then_inc(turned, 1)
                pe.wait_ge(scaled, 6)
                for n, (first, rows) in enumerate(TOK):
                    for r in range(2):
                        last = nc.tensor.transpose(banks[0:rows, 3 + n // 2, (n % 2) * 256 + r * P:(n % 2) * 256 + (r + 1) * P],
                                                   k.ckvT[:, r, first:first + rows], k.col("ident"))
                last.then_inc(turned, 1)
                pe.wait_ge(rotated, 3)
                for n, (first, rows) in enumerate(TOK):
                    last = nc.tensor.transpose(banks[0:ROPE, 5, first:first + rows], k.kpe_tm[0:rows, n, :], k.col("ident", 0, rows, rows))
                last.then_inc(back, 1)

            @block.scalar
            def _(act):
                def round_weights(i):
                    act.wait_ge(loaded[i], 16 if i < 3 else 32)
                    if i >= 2:
                        act.wait_ge(made, 2 * i - 2)
                    n = 2 * P if i < 3 else P
                    nc.scalar.copy(heads[:, i % 2, :, 0:n], ring[:, i, :, 0:n]).then_inc(rounded, 1)
                round_weights(0)
                round_weights(1)
                for i in range(6):
                    if i in (2, 4):
                        round_weights(i // 2 + 1)
                    act.wait_ge(made, i + 1)
                    dst = k.cqT[:, i, :] if i < 4 else k.ckvT[:, i - 4, :]
                    nc.scalar.copy(dst, banks[:, i, 0:T]).then_inc(kept, 1)
                    nc.scalar.activation(sq[:, i, :], banks[:, i, 0:T], ACT.Square).then_inc(squared, 1)
                act.wait_ge(made, 7)
                nc.scalar.copy(kpeT[:, :], banks[0:ROPE, 6, 0:T]).then_inc(kept, 1)
                for n, width in enumerate((QRANK, KVRANK)):
                    act.wait_ge(summed, n + 1)
                    nc.scalar.activation(inv[:, n, :], banks[:, n, 0:T], ACT.Ln, bias=k.col("eps"), scale=1.0 / width).then_inc(inverse, 1)
                act.wait_ge(inverse, 2)
                nc.scalar.activation(inv[:, :, :], inv[:, :, :], ACT.Exp, scale=-0.5).then_inc(inverse, 1)
                act.wait_ge(turned, 2)
                nc.scalar.copy(lat_tm[:, 0:2, :], banks[:, 3, :].rearrange("p (n r) -> p n r", n=2)).then_inc(lat_kept, 1)
                nc.scalar.copy(lat_tm[0:NSAM, 2, :], banks[0:NSAM, 4, 0:KVRANK]).then_inc(lat_kept, 1)
                act.wait_ge(lat_kept, 2)
                nc.scalar.copy(k.new_c[0:NSAM, :], lat_tm[0:NSAM, 2, :])
                act.wait_ge(back, 1)
                nc.scalar.copy(k.kpe_rT[:, :], banks[0:ROPE, 5, 0:T]).then_inc(back_kept, 1)

            @block.vector
            def _(dve):
                c = Chain(dve, step)
                for i in range(4):
                    dve.wait_ge(rounded, i + 1)
                    n = 2 * P if i < 3 else P
                    nc.vector.tensor_tensor(rests[:, i % 2, :, 0:n], ring[:, i, :, 0:n], heads[:, i % 2, :, 0:n].bitcast(F32),
                                            ALU.subtract).then_inc(split, 1)
                dve.wait_ge(turned, 1)
                for n, (first, rows) in enumerate(TOK):
                    x = banks[0:rows, 2, n * ROPE:(n + 1) * ROPE]
                    cos, sin = k.col("cos", 32 * n, 32, rows), k.col("sin", 32 * n, 32, rows)
                    p = rot[0:rows, n, :, :]
                    nc.vector.tensor_tensor(p[:, 0, :], x[:, 0:32], cos, ALU.mult)
                    nc.vector.tensor_tensor(p[:, 1, :], x[:, 32:64], sin, ALU.mult)
                    nc.vector.tensor_tensor(p[:, 2, :], x[:, 0:32], sin, ALU.mult)
                    c(nc.vector.tensor_tensor(p[:, 3, :], x[:, 32:64], cos, ALU.mult))
                    nc.vector.tensor_tensor(k.kpe_tm[0:rows, n, 0:32], p[:, 0, :], p[:, 1, :], ALU.subtract)
                    nc.vector.tensor_tensor(k.kpe_tm[0:rows, n, 32:64], p[:, 2, :], p[:, 3, :], ALU.add).then_inc(rotated, 1)
                dve.wait_ge(inverse, 3)
                for i in range(6):
                    buf, j, gain = (k.cqT, i, "mla_q_a_g") if i < 4 else (k.ckvT, i - 4, "mla_kv_a_g")
                    nc.vector.scalar_tensor_tensor(buf[:, j, :], buf[:, j, :], k.par(gain, j), inv[:, i // 4, :],
                                                   ALU.mult, ALU.mult).then_inc(scaled, 1)


def mla_qkv(nc, k):
    with Stage(nc) as st:
        w_q = st.sb("w_q_b", [P, 4, HEADS * QK])
        q_tm = st.sb("q_tm", [P, HEADS, QK])
        k_tm = st.sb("k_tm", [P, HEADS, QK])
        sq = st.sb("qk_sq", [P, HEADS, QK])
        rot = st.sb("q_rope_products", [P, 4, HEADS, 32])
        gain = st.sb("qk_gain", [P, QK])
        ss = st.sb("qk_sumsq", [P, 2, HEADS])
        banks = st.ps("qkv_banks", [P, 8, BANK])
        loaded, made, step = st.sem("weights_loaded"), st.sem("rows_made"), st.sem("dve_step")
        q_kept, k_kept, v_kept = st.sem("q_kept"), st.sem("k_kept"), st.sem("v_kept")
        q_sq, k_sq = st.sem("q_squared"), st.sem("k_squared")
        q_rope, q_sum, k_sum, q_inv, k_inv = (st.sem(n) for n in ("q_rotated", "q_summed", "k_summed", "q_inverse", "k_inverse"))
        q_norm, k_norm = st.sem("q_normed"), st.sem("k_normed")
        turned, t_kept = st.sem("bank_turned"), st.sem("bank_kept")
        with st.block() as block:
            @block.sync
            def _(sp):
                sp.dma_start(w_q[:, :, :], k.ldram("mla_w_q_b").rearrange("(t p) h e -> p t (h e)", p=P)).then_inc(loaded, 16)
                sp.dma_start(k.w_kb[:, :, :], k.ldram("mla_w_kb").rearrange("(t p) h e -> p t (h e)", p=P)).then_inc(loaded, 16)
                sp.dma_start(k.w_vb[:, :, :], k.ldram("mla_w_vb").rearrange("(t p) h e -> p t (h e)", p=P)).then_inc(loaded, 16)

            def groups(n):
                out = []
                for half in range(2):
                    out += [("q", 0, half), ("q", 1, half)]
                    if n < 2:
                        out += [("k", 0, half), ("k", 1, half)]
                return out

            @block.tensor
            def _(pe):
                pe.wait_ge(loaded, 48)
                g_total = 0
                for n, (first, rows) in enumerate(TOK):
                    if n:
                        pe.wait_ge(q_kept, n)
                        pe.wait_ge(k_kept, n)
                        pe.wait_ge(v_kept, n)
                        pe.wait_ge(t_kept, g_total)
                    for j in range(3):
                        for t in range(4):
                            last = nc.tensor.matmul(banks[0:rows, j, :], k.cqT[:, t, first:first + rows], w_q[:, t, j * 512:(j + 1) * 512],
                                                    start=t == 0, stop=t == 3)
                    last.then_inc(made, 1)
                    if n < 2:
                        for b0, w in ((3, k.w_kb), (5, k.w_vb)):
                            for j in range(2):
                                for t in range(2):
                                    last = nc.tensor.matmul(banks[:, b0 + j, :], k.ckvT[:, t, first:first + rows], w[:, t, j * 512:(j + 1) * 512],
                                                            start=t == 0, stop=t == 1)
                            last.then_inc(made, 1)
                    for what, part, half in groups(n):
                        if what == "q" and part == 0 and half == 0:
                            pe.wait_ge(q_norm, n + 1)
                        if what == "k" and part == 0 and half == 0:
                            pe.wait_ge(k_norm, n + 1)
                        if g_total >= 1:
                            pe.wait_ge(t_kept, g_total)
                        src = q_tm if what == "q" else k_tm
                        for i in range(4):
                            h = 4 * half + i
                            e = slice(0, NOPE) if part == 0 else slice(NOPE, QK)
                            last = nc.tensor.transpose(banks[0:(NOPE if part == 0 else ROPE), 7, i * P:i * P + rows],
                                                       src[0:rows, h, e], k.col("ident", 0, rows, rows))
                        last.then_inc(turned, 1)
                        g_total += 1

            @block.scalar
            def _(act):
                m, g_total = 0, 0
                for n, (first, rows) in enumerate(TOK):
                    act.wait_ge(made, m + 1)
                    if n:
                        act.wait_ge(t_kept, g_total)
                    nc.scalar.copy(q_tm[0:rows, :, :].rearrange("p h e -> p (h e)"), banks[0:rows, 0:3, :]).then_inc(q_kept, 1)
                    if n < 2:
                        act.wait_ge(made, m + 2)
                        nc.scalar.copy(k_tm[:, :, 0:NOPE], banks[:, 3:5, :].rearrange("p a (h e) -> p (a h) e", e=NOPE)).then_inc(k_kept, 1)
                        act.wait_ge(made, m + 3)
                        nc.scalar.copy(k.v_tm[:, n, :], banks[:, 5:7, :]).then_inc(v_kept, 1)
                        m += 3
                    act.wait_ge(q_rope, n + 1)
                    nc.scalar.activation(sq[0:rows, :, :], q_tm[0:rows, :, :], ACT.Square).then_inc(q_sq, 1)
                    act.wait_ge(q_sum, n + 1)
                    nc.scalar.activation(ss[0:rows, 0, :], ss[0:rows, 0, :], ACT.Ln, bias=k.col("eps", rows=rows), scale=1.0 / QK).then_inc(q_inv, 1)
                    act.wait_ge(q_inv, 2 * n + 1)
                    nc.scalar.activation(ss[0:rows, 0, :], ss[0:rows, 0, :], ACT.Exp, scale=-0.5).then_inc(q_inv, 1)
                    if n < 2:
                        nc.scalar.activation(sq[:, :, :], k_tm[:, :, :], ACT.Square).then_inc(k_sq, 1)
                        act.wait_ge(k_sum, n + 1)
                        nc.scalar.activation(ss[:, 1, :], ss[:, 1, :], ACT.Ln, bias=k.col("eps"), scale=1.0 / QK).then_inc(k_inv, 1)
                        act.wait_ge(k_inv, 2 * n + 1)
                        nc.scalar.activation(ss[:, 1, :], ss[:, 1, :], ACT.Exp, scale=-0.5).then_inc(k_inv, 1)
                    for what, part, half in groups(n):
                        act.wait_ge(turned, g_total + 1)
                        r = NOPE if part == 0 else ROPE
                        dst = ((k.qnT, k.qrT), (k.knT, k.krT))[what == "k"][part]
                        nc.scalar.copy(dst[0:r, 4 * half:4 * half + 4, first:first + rows],
                                       banks[0:r, 7, :].rearrange("p (i t) -> p i t", i=4)[:, :, 0:rows]).then_inc(t_kept, 1)
                        g_total += 1

            @block.vector
            def _(dve):
                c = Chain(dve, step)
                c(nc.vector.scalar_tensor_tensor(gain[:, :], k.q_gain[:, :], QK ** -0.5, k.k_gain[:, :], ALU.mult, ALU.mult))
                for n, (first, rows) in enumerate(TOK):
                    q = q_tm[0:rows, :, :]
                    cos = k.col("cos", 32 * n, 32, rows).unsqueeze(1).to_broadcast([rows, HEADS, 32])
                    sin = k.col("sin", 32 * n, 32, rows).unsqueeze(1).to_broadcast([rows, HEADS, 32])
                    r = rot[0:rows, :, :, :]
                    x1, x2 = q[:, :, NOPE:NOPE + 32], q[:, :, NOPE + 32:QK]
                    dve.wait_ge(q_kept, n + 1)
                    nc.vector.tensor_tensor(r[:, 0, :, :], x1, cos, ALU.mult)
                    nc.vector.tensor_tensor(r[:, 1, :, :], x2, sin, ALU.mult)
                    nc.vector.tensor_tensor(r[:, 2, :, :], x1, sin, ALU.mult)
                    c(nc.vector.tensor_tensor(r[:, 3, :, :], x2, cos, ALU.mult))
                    if n < 2:
                        dve.wait_ge(k_kept, n + 1)
                        c(nc.vector.tensor_copy(k_tm[:, :, NOPE:QK], k.kpe_tm[:, n:n + 1, :].to_broadcast([P, HEADS, ROPE])))
                    c(nc.vector.tensor_tensor(x1, r[:, 0, :, :], r[:, 1, :, :], ALU.subtract))
                    nc.vector.tensor_tensor(x2, r[:, 2, :, :], r[:, 3, :, :], ALU.add).then_inc(q_rope, 1)
                    dve.wait_ge(q_sq, n + 1)
                    nc.vector.tensor_reduce(ss[0:rows, 0, :], sq[0:rows, :, :], AX.X, ALU.add).then_inc(q_sum, 1)
                    dve.wait_ge(q_inv, 2 * n + 2)
                    c(nc.vector.tensor_tensor(q, q, bc(ss[0:rows, 0, :], QK), ALU.mult))
                    nc.vector.tensor_tensor(q, q, gain[0:rows, :].unsqueeze(1).to_broadcast([rows, HEADS, QK]), ALU.mult).then_inc(q_norm, 1)
                    if n < 2:
                        dve.wait_ge(k_sq, n + 1)
                        nc.vector.tensor_reduce(ss[:, 1, :], sq[:, :, :], AX.X, ALU.add).then_inc(k_sum, 1)
                        dve.wait_ge(k_inv, 2 * n + 2)
                        nc.vector.tensor_tensor(k_tm[:, :, :], k_tm[:, :, :], bc(ss[:, 1, :], QK), ALU.mult).then_inc(k_norm, 1)


def mla_prompt(nc, k):
    with Stage(nc) as st:
        s = st.sb("scores", [P, 2, 384])
        pT = st.sb("probs_T", [P, 2, 384])
        top, den = st.sb("score_max", [P, 2, 2]), st.sb("prob_sum", [P, 2, 2])
        banks = st.ps("attn_banks", [P, 6, BANK])
        scored, masked, peaked, exped = (st.sem(n) for n in ("scored", "masked", "max_ready", "exp_ready"))
        normed, turned, t_kept, out, o_kept, step = (st.sem(n) for n in ("probs_normed", "probs_turned", "probs_T_ready", "head_made", "head_kept", "dve_step"))
        spans = ((0, 128), (128, 384))
        with st.block() as block:
            @block.tensor
            def _(pe):
                def score(h):
                    b = h % 2
                    if h >= 2:
                        pe.wait_ge(masked, h - 1)
                    for qt, (a, z) in enumerate(spans):
                        o = banks[:, b, a:z]
                        qs = slice(qt * P, (qt + 1) * P)
                        nc.tensor.matmul(o, k.qnT[:, h, qs], k.knT[:, h, 0:z - a], start=True, stop=False, skip_group_check=True)
                        last = nc.tensor.matmul(o, k.qrT[:, h, qs], k.krT[:, h, 0:z - a], start=False, stop=True, skip_group_check=True)
                    last.then_inc(scored, 1)
                score(0)
                for h in range(HEADS):
                    if h + 1 < HEADS:
                        score(h + 1)
                    b = h % 2
                    pe.wait_ge(normed, h + 1)
                    if h >= 2:
                        pe.wait_ge(t_kept, h - 1)
                    for j in range(3):
                        last = nc.tensor.transpose(banks[:, 2 + b, j * P:(j + 1) * P], s[:, b, j * P:(j + 1) * P], k.col("ident"))
                    last.then_inc(turned, 1)
                    pe.wait_ge(t_kept, h + 1)
                    if h >= 2:
                        pe.wait_ge(o_kept, h - 1)
                    for j, (col, key, start, stop) in enumerate(((0, 0, True, True), (1, 0, True, False), (1, 1, False, True))):
                        last = nc.tensor.matmul(banks[:, 4 + b, col * P:(col + 1) * P], k.v_tm[:, key, h * P:(h + 1) * P],
                                                pT[:, b, j * P:(j + 1) * P], start=start, stop=stop, skip_group_check=True)
                    last.then_inc(out, 1)

            @block.scalar
            def _(act):
                for h in range(HEADS):
                    b = h % 2
                    act.wait_ge(peaked, h + 1)
                    for qt, (a, z) in enumerate(spans):
                        last = nc.scalar.activation(s[:, b, a:z], s[:, b, a:z], ACT.Exp, bias=top[:, b, qt:qt + 1], accum_out=den[:, b, qt:qt + 1])
                    last.then_inc(exped, 1)
                    act.wait_ge(turned, h + 1)
                    nc.scalar.copy(pT[:, b, :], banks[:, 2 + b, 0:384]).then_inc(t_kept, 1)
                    act.wait_ge(out, h + 1)
                    nc.scalar.copy(k.o_mla[:, h, 0:SEQ], banks[:, 4 + b, 0:SEQ]).then_inc(o_kept, 1)

            @block.vector
            def _(dve):
                c = Chain(dve, step)
                causal = k.col("causal", 0, P)
                for h in range(HEADS):
                    b = h % 2
                    dve.wait_ge(scored, h + 1)
                    if h >= 2:
                        dve.wait_ge(turned, h - 1)
                    nc.vector.tensor_tensor(s[:, b, 0:P], banks[:, b, 0:P], causal, ALU.add)
                    nc.vector.tensor_copy(s[:, b, P:2 * P], banks[:, b, P:2 * P])
                    nc.vector.tensor_tensor(s[:, b, 2 * P:3 * P], banks[:, b, 2 * P:3 * P], causal, ALU.add).then_inc(masked, 1)
                    dve.wait_ge(masked, h + 1)
                    for qt, (a, z) in enumerate(spans):
                        last = nc.vector.tensor_reduce(top[:, b, qt:qt + 1], s[:, b, a:z], AX.X, ALU.max)
                    c(last)
                    nc.vector.tensor_scalar(top[:, b, :], top[:, b, :], -1.0, None, ALU.mult).then_inc(peaked, 1)
                    dve.wait_ge(exped, h + 1)
                    c(nc.vector.reciprocal(den[:, b, :], den[:, b, :]))
                    for qt, (a, z) in enumerate(spans):
                        last = nc.vector.tensor_scalar(s[:, b, a:z], s[:, b, a:z], den[:, b, qt:qt + 1], None, ALU.mult)
                    last.then_inc(normed, 1)


def mla_absorb(nc, k):
    with Stage(nc) as st:
        kbT = st.sb("w_kb_T", [P, HEADS, KVRANK])
        sq = st.sb("new_key_sq", [NSAM, HEADS * NOPE])
        sqp = st.sb("new_rope_sq", [NSAM, ROPE])
        ss, ssp = st.sb("new_key_sumsq", [NSAM, HEADS]), st.sb("new_rope_sumsq", [NSAM, 1])
        mask = st.sb("new_mask", [NSAM, NSAM])
        banks = st.ps("absorb_banks", [P, 8, BANK])
        turned, t_kept, made, qa_kept = st.sem("kb_turned"), st.sem("kb_T_kept"), st.sem("qa_made"), st.sem("qa_kept")
        new_made, squared, summed, inverse, step = (st.sem(n) for n in ("new_keys_made", "new_squared", "new_summed", "new_inverse", "dve_step"))
        page_in = st.sem("page_table_loaded")
        with st.block() as block:
            @block.sync
            def _(sp):
                sp.dma_start(k.pages[:, :], k.d["page_table"].rearrange("b (o n) -> o (b n)", o=1)).then_inc(page_in, 16)
                sp.wait_ge(page_in, 16)

            @block.tensor
            def _(pe):
                for r in range(2):
                    for half in range(2):
                        for i in range(4):
                            last = nc.tensor.transpose(banks[:, 2 * r + half, i * P:(i + 1) * P],
                                                       k.w_kb[:, r, (4 * half + i) * P:(4 * half + i + 1) * P], k.col("ident"))
                        last.then_inc(turned, 1)
                for j in range(2):
                    for t in range(2):
                        last = nc.tensor.matmul(banks[0:NSAM, 5 + j, :], k.ckvT[:, t, SEQ:T], k.w_kb[:, t, j * 512:(j + 1) * 512],
                                                start=t == 0, stop=t == 1)
                last.then_inc(new_made, 1)
                pe.wait_ge(t_kept, 4)
                for r in range(2):
                    for h in range(HEADS):
                        last = nc.tensor.matmul(banks[:, 4, r * 256 + h * NSAM:r * 256 + (h + 1) * NSAM], kbT[:, h, r * P:(r + 1) * P],
                                                k.qnT[:, h, SEQ:T], start=True, stop=True, skip_group_check=True)
                last.then_inc(made, 1)
                pe.wait_ge(qa_kept, 3)
                for r in range(2):
                    nc.tensor.matmul(banks[0:NSAM, 7, 0:256], k.ckvT[:, r, SEQ:T], k.qa[:, r, :, :].rearrange("p b c -> p (b c)"),
                                     start=r == 0, stop=False)
                nc.tensor.matmul(banks[0:NSAM, 7, 0:256], k.kpe_rT[:, SEQ:T], k.qr[:, :, :].rearrange("p b c -> p (b c)"),
                                 start=False, stop=True).then_inc(new_made, 1)

            @block.scalar
            def _(act):
                for r in range(2):
                    for half in range(2):
                        act.wait_ge(turned, 2 * r + half + 1)
                        nc.scalar.copy(kbT[:, 4 * half:4 * half + 4, r * P:(r + 1) * P],
                                       banks[:, 2 * r + half, :].rearrange("p (i n) -> p i n", n=P)).then_inc(t_kept, 1)
                act.wait_ge(new_made, 1)
                nc.scalar.activation(sq[:, :], banks[0:NSAM, 5:7, :], ACT.Square).then_inc(squared, 1)
                nc.scalar.activation(sqp[:, :], k.kpe_tm[0:NSAM, 2, :], ACT.Square, accum_out=ssp[:, :]).then_inc(squared, 1)
                act.wait_ge(summed, 1)
                nc.scalar.activation(ss[:, :], ss[:, :], ACT.Ln, bias=k.col("eps", rows=NSAM), scale=1.0 / QK).then_inc(inverse, 1)
                act.wait_ge(inverse, 1)
                nc.scalar.activation(ss[:, :], ss[:, :], ACT.Exp, scale=-0.5).then_inc(inverse, 1)

            @block.vector
            def _(dve):
                c = Chain(dve, step)
                nc.vector.memset(k.new_c[NSAM:2 * NSAM, :], 0.0)
                nc.vector.memset(k.new_c[2 * NSAM:P, :], 0.0)
                nc.vector.memset(k.new_scores[:, :, :], -1e30)
                c(nc.vector.tensor_scalar(mask[:, :], k.col("segtri", rows=NSAM), -1.0, 1e30, ALU.add, ALU.mult))
                dve.wait_ge(made, 1)
                for r in range(2):
                    nc.vector.tensor_copy(k.qa[:, r, :, :].rearrange("p b (h t) -> p h b t", h=HEADS),
                                          banks[:, 4, r * 256:(r + 1) * 256].rearrange("p (h b t) -> p h b t", h=HEADS, b=NB)).then_inc(qa_kept, 1)
                nc.vector.tensor_copy(k.qr[:, :, :].rearrange("p b (h t) -> p h b t", h=HEADS),
                                      k.qrT[:, :, SEQ:T].rearrange("p h (b t) -> p h b t", b=NB)).then_inc(qa_kept, 1)
                dve.wait_ge(squared, 2)
                c(nc.vector.tensor_reduce(ss[:, :], sq[:, :].rearrange("p (h e) -> p h e", e=NOPE), AX.X, ALU.add))
                nc.vector.tensor_scalar(ss[:, :], ss[:, :], ssp[:, 0:1], None, ALU.add).then_inc(summed, 1)
                dve.wait_ge(inverse, 2)
                dve.wait_ge(new_made, 2)
                for b in range(NB):
                    out = k.new_scores[0:NSAM, b, :].rearrange("p (h t) -> p h t", h=HEADS)
                    last = nc.vector.tensor_tensor(out, banks[0:NSAM, 7, b * 32:(b + 1) * 32].rearrange("p (h t) -> p h t", h=HEADS),
                                                   bc(ss[:, :], NS), ALU.mult)
                c(last)
                for b in range(NB):
                    out = k.new_scores[0:NSAM, b, :].rearrange("p (h t) -> p h t", h=HEADS)
                    last = nc.vector.tensor_tensor(out, out, mask[:, b * NS:(b + 1) * NS].unsqueeze(1).to_broadcast([NSAM, HEADS, NS]), ALU.add)
                c(last)


def rwkv_sample_rows(nc, k):
    with Stage(nc) as st:
        rows = st.sb("sample_rows", [NSAM, 6, D])
        banks = st.ps("sample_banks", [P, 8, BANK])
        turned, kept, out, back = st.sem("rows_turned"), st.sem("rows_kept"), st.sem("rows_stored"), st.sem("rows_back")
        with st.block() as block:
            @block.tensor
            def _(pe):
                for g in range(12):
                    if g >= 8:
                        pe.wait_ge(kept, g - 7)
                    for i in range(4):
                        last = nc.tensor.transpose(banks[0:NSAM, g % 8, i * P:(i + 1) * P], k.samT[:, g // 2, 4 * (g % 2) + i, :], k.col("ident"))
                    last.then_inc(turned, 1)

            @block.vector
            def _(dve):
                for g in range(12):
                    dve.wait_ge(turned, g + 1)
                    nc.vector.tensor_copy(rows[:, g // 2, g % 2 * 512:(g % 2 + 1) * 512], banks[0:NSAM, g % 8, :]).then_inc(kept, 1)

            @block.sync
            def _(sp):
                sp.wait_ge(kept, 12)
                sp.dma_start(k.d["scratch_vec"].rearrange("t n d -> t n d"), rows[:, :, :]).then_inc(out, 16)
                sp.wait_ge(out, 16)
                for b in range(NB):
                    for n in range(6):
                        sp.dma_start(k.vec[16 * b:16 * b + 16, n, :, :],
                                     k.d["scratch_vec"][NS * b:NS * b + NS, n, :].rearrange("t (h d) -> h t d", d=64)).then_inc(back, 16)
                sp.dma_start(k.state[:, :, :], k.ldram("state_rwkv").rearrange("b h v k -> (b h) v k")).then_inc(back, 16)
                sp.wait_ge(back, 16 * (6 * NB + 1))


def rwkv_sample_pool(nc, k, pool, step):
    c = Chain(pool, step)
    S, tmp = k.state[:, :, :], k.state_tmp[:, :, :]
    full = [P, 64, 64]

    def over_v(n, t):
        return k.vec[:, n, t:t + 1, :].to_broadcast(full)
    R, W, K, V, KK, KKA = range(6)

    def dot(out, n, t):
        c(nc.gpsimd.tensor_tensor(tmp, S, over_v(n, t), ALU.mult))
        w = 32
        while w >= 2:
            c(nc.gpsimd.tensor_tensor(tmp[:, :, 0:w], tmp[:, :, 0:w], tmp[:, :, w:2 * w], ALU.add))
            w //= 2
        c(nc.gpsimd.tensor_tensor(out, tmp[:, :, 0], tmp[:, :, 1], ALU.add))
    for t in range(NS):
        dot(k.vec_sa[:, :], KK, t)
        c(nc.gpsimd.tensor_tensor(S, S, over_v(W, t), ALU.mult))
        c(nc.gpsimd.tensor_tensor(tmp, bc(k.vec_sa[:, :], 64), over_v(KKA, t), ALU.mult))
        c(nc.gpsimd.tensor_tensor(S, S, tmp, ALU.subtract))
        c(nc.gpsimd.tensor_tensor(tmp, bc(k.vec[:, V, t, :], 64), over_v(K, t), ALU.mult))
        c(nc.gpsimd.tensor_tensor(S, S, tmp, ALU.add))
        dot(k.vec_y[:, t, :], R, t)
    return c.n


POOL_STEPS = NS * (2 * 7 + 5)


def cache_attention(nc, k):
    J = PAGES + 1
    LAST = NB - 1
    ROPE_AT = (10, 13)
    TOTAL, LN, EXP, SCALE, TOP, TURN_TOP, SPREAD, SOFT, PART, VALUES = 0, 1, 2, 3, 4, 5, 6, 7, 8, 9
    with Stage(nc) as st:
        lat = st.sb("latents", [P, 2, PAGES, KVRANK])
        kpe = st.sb("rope_keys", [P, 2, PAGES, ROPE])
        ch, cl = st.sb("latent_T_head", [P, 2, KVRANK], F32R), st.sb("latent_T_rest", [P, 2, KVRANK], F32R)
        wh, wl = st.sb("w_kb_head", [P, 2, HEADS * NOPE], F32R), st.sb("w_kb_rest", [P, 2, HEADS * NOPE], F32R)
        qh, ql = st.sb("qa_head", [P, 2, NB, 32], F32R), st.sb("qa_rest", [P, 2, NB, 32], F32R)
        free = k.w_kb[:, :, :].rearrange("p a b -> p (a b)")
        def reuse(first, *shape):
            n = int(np.prod(shape))
            letters = "abc"[:len(shape)]
            spaced = " ".join(letters)
            return free[:, first:first + n].rearrange(f"p ({spaced}) -> p {spaced}", **dict(zip(letters, shape)))
        s = reuse(0, 2, J, 32)
        ss = reuse(1088, 2, PAGES, HEADS)
        kpT = reuse(1344, 2, P)[0:ROPE, :, :]
        top, psum_p, inv, diag = (reuse(1600 + 32 * n, 1, 32)[:, 0, :] for n in range(4))
        diag = diag[0:32, :]
        kpe_sq = k.samT[:, 0:2, :, :].rearrange("p a b c -> p (a b c)").rearrange("p (j c) -> p j c", c=ROPE)
        sq = st.sb("key_sq", [P, 2, HEADS * NOPE])
        ssp = st.sb("rope_sumsq", [P, PAGES])
        peak = st.sb("query_max", [32, 1])
        acc = k.qa
        kbank = st.ps("key_banks", [P, 4, BANK])
        xbank = st.ps("turn_bank", [P, BANK])
        sbank = st.ps("score_banks", [P, 2, BANK])
        mbank = st.ps("misc_bank", [P, BANK])
        in_l = [[st.sem(f"latents_loaded{i}_{g}") for g in range(4)] for i in range(2)]
        w_heads, w_split = st.sem("weight_heads_ready"), st.sem("weights_split")
        turned, headed, t_kept, keyed, scored, squared, summed = (st.sem(n) for n in (
            "page_turned", "page_head_ready", "page_T_ready", "page_keys_made", "page_scored", "page_squared", "page_summed"))
        rope_sq, rope_sum, tot, inverse = (st.sem(n) for n in ("rope_squared", "rope_summed", "sumsq_total", "inverse_root"))
        scaled, topped, top_turned, peaked, spread, shifted, exped = (st.sem(n) for n in (
            "scores_scaled", "page_max_ready", "max_turned", "max_diag_ready", "max_spread", "scores_shifted", "exp_ready"))
        part, outed, divided, vmade, step = (st.sem(n) for n in ("prob_parts_summed", "latent_sums_made", "latent_out_ready", "values_made", "dve_step"))
        pool_step, rwkv_out = st.sem("pool_step"), st.sem("rwkv_rows_stored")

        def seqs(eng, body, finish):
            body(0, 0, 0)
            with eng.Fori(0, NB // 2 - 1) as i:
                body(i * 2 + 1, 1, i)
                body(i * 2 + 2, 0, i + 1)
            body(LAST, 1, NB // 2 - 1)
            for at in range(TOTAL, VALUES + 1):
                finish(LAST, 1, at)

        def is_first(b):
            return isinstance(b, int) and b == 0

        def is_last(b):
            return isinstance(b, int) and b == LAST

        with st.block() as block:
            @block.sync
            def _(sp):
                def load(b, slot):
                    for j in range(PAGES):
                        page = sp.value_load(k.pages[0:1, ds(b * PAGES + j, 1)], min_val=0, max_val=NPOOL - 1)
                        row = ds(page, 1)
                        sp.dma_start(lat[:, slot, j, :], k.ldram("cache_kv_latent")[row].rearrange("o p r -> (o p) r")).then_inc(in_l[slot][j // 4], 16)
                        sp.dma_start(kpe[:, slot, j, :], k.ldram("cache_k_rope")[row].rearrange("o p r -> (o p) r")).then_inc(in_l[slot][j // 4], 16)
                load(0, 0)
                load(1, 1)
                with sp.Fori(1, NB // 2) as i:
                    for slot in range(2):
                        sp.wait_ge(outed, i * 2 + (slot - 1))
                        load(i * 2 + slot, slot)
                sp.wait_ge(pool_step, POOL_STEPS)
                sp.dma_start(k.ldram("s_rwkv").rearrange("b h v k -> (b h) v k"), k.state[:, :, :]).then_inc(rwkv_out, 16)
                sp.wait_ge(rwkv_out, 16)

            @block.gpsimd
            def _(pool):
                assert rwkv_sample_pool(nc, k, pool, pool_step) == POOL_STEPS

            @block.tensor
            def _(pe):
                def turn(b, slot, uses, j):
                    if j % 4 == 0:
                        pe.wait_ge(in_l[slot][j // 4], uses * 128 + 128)
                    if not (is_first(b) and j == 0):
                        pe.wait_ge(t_kept, b * PAGES + j)
                    for r in range(2):
                        nc.tensor.transpose(xbank[:, r * P:(r + 1) * P], lat[:, slot, j, r * P:(r + 1) * P], k.col("ident"))
                    nc.tensor.transpose(xbank[0:ROPE, 2 * P:3 * P], kpe[:, slot, j, :], k.col("ident")).then_inc(turned, 1)

                def body(b, slot, uses):
                    base = b * PAGES
                    for j in range(PAGES):
                        x = j % 2
                        pe.wait_ge(t_kept, base + (j + 1))
                        if j + 1 < PAGES:
                            turn(b, slot, uses, j + 1)
                        elif not is_last(b):
                            turn(b + 1, 1 - slot, uses + slot, 0)
                        if not (is_first(b) and j < 2):
                            pe.wait_ge(squared, base + (j - 1))
                        o = sbank[:, slot, j * 32:(j + 1) * 32]
                        for r in range(2):
                            for c, n, parts in ((ch, 0, ((wh, qh), (wl, ql))), (cl, 1, ((wh, qh),))):
                                lhsT = c[:, x, r * P:(r + 1) * P]
                                for w, q in parts:
                                    start, stop = r == 0 and n == 0 and w is wh, r == 1 and n == 1
                                    for half in range(2):
                                        last = nc.tensor.matmul(kbank[:, 2 * x + half, :], lhsT, w[:, r, half * 512:(half + 1) * 512],
                                                                start=start, stop=stop)
                                    if stop:
                                        last.then_inc(keyed, 1)
                                    nc.tensor.matmul(o, lhsT, q[:, r, ds(b, 1), :].rearrange("p o c -> p (o c)"),
                                                     start=start, stop=False, skip_group_check=True)
                        nc.tensor.matmul(o, kpT[:, x, :], k.qr[:, ds(b, 1), :].rearrange("p o c -> p (o c)"),
                                         start=False, stop=True, skip_group_check=True).then_inc(scored, 1)
                        if not is_first(b):
                            finish(b - 1, 1 - slot, j)

                def finish(b, slot, at):
                    if at == TURN_TOP:
                        pe.wait_ge(topped, b + 1)
                        nc.tensor.transpose(mbank[0:32, 128:256], top[:, :], k.col("ident")).then_inc(top_turned, 1)
                    if at == SPREAD:
                        pe.wait_ge(peaked, b + 1)
                        nc.tensor.matmul(mbank[:, 256:288], k.const[0:32, CCOL["ones"][0]:CCOL["ones"][0] + P], diag[:, :],
                                         start=True, stop=True, skip_group_check=True).then_inc(spread, 1)
                    if at == VALUES:
                        pe.wait_ge(part, b + 1)
                        nc.tensor.matmul(mbank[:, 64:96], k.col("ones"), psum_p[:, :], start=True, stop=True, skip_group_check=True)
                        for r in range(2):
                            for j in range(J):
                                c = lat[:, slot, j, r * P:(r + 1) * P] if j < PAGES else k.new_c[:, r * P:(r + 1) * P]
                                last = nc.tensor.matmul(mbank[:, r * 32:(r + 1) * 32], c, s[:, slot, j, :], start=j == 0, stop=j == J - 1,
                                                        skip_group_check=True)
                        last.then_inc(outed, 1)
                turn(0, 0, 0, 0)
                pe.wait_ge(w_split, 2)
                seqs(pe, body, finish)
                pe.wait_ge(divided, NB)
                for h in range(HEADS):
                    for r in range(2):
                        last = nc.tensor.matmul(mbank[:, 256 + h * 32:256 + (h + 1) * 32], k.w_vb[:, r, h * P:(h + 1) * P],
                                                acc[:, r, :, h * NS:(h + 1) * NS], start=r == 0, stop=r == 1, skip_group_check=True)
                last.then_inc(vmade, 1)

            @block.scalar
            def _(act):
                nc.scalar.copy(wh[:, :, :], k.w_kb[:, :, :]).then_inc(w_heads, 1)
                nc.scalar.copy(qh[:, :, :, :], k.qa[:, :, :, :]).then_inc(w_heads, 1)

                act.wait_ge(w_split, 2)

                def head(b, j):
                    x = j % 2
                    act.wait_ge(turned, b * PAGES + (j + 1))
                    if not (is_first(b) and j < 2):
                        act.wait_ge(scored, b * PAGES + (j - 1))
                    nc.scalar.copy(ch[:, x, :], xbank[:, 0:2 * P])
                    nc.scalar.copy(kpT[:, x, :], xbank[0:ROPE, 2 * P:3 * P]).then_inc(headed, 1)

                def body(b, slot, uses):
                    base = b * PAGES
                    for j in range(PAGES):
                        x = j % 2
                        if j + 2 < PAGES:
                            head(b, j + 2)
                        elif not is_last(b):
                            head(b + 1, j + 2 - PAGES)
                        act.wait_ge(keyed, base + (j + 1))
                        if not (is_first(b) and j < 2):
                            act.wait_ge(summed, base + (j - 1))
                        nc.scalar.activation(sq[:, x, :], kbank[:, 2 * x:2 * x + 2, :], ACT.Square).then_inc(squared, 1)
                        if j in ROPE_AT:
                            half = ROPE_AT.index(j)
                            for g in range(2 * half, 2 * half + 2):
                                act.wait_ge(in_l[slot][g], uses * 128 + 128)
                            if not (is_first(b) and half == 0):
                                act.wait_ge(rope_sum, b * 2 + half)
                            nc.scalar.activation(kpe_sq[:, :, :], kpe[:, slot, 8 * half:8 * half + 8, :], ACT.Square).then_inc(rope_sq, 1)
                        if not is_first(b):
                            finish(b - 1, 1 - slot, j)

                def finish(b, slot, at):
                    if at == LN:
                        act.wait_ge(tot, b + 1)
                        nc.scalar.activation(ss[:, slot, :, :], ss[:, slot, :, :], ACT.Ln, bias=k.col("eps"), scale=1.0 / QK).then_inc(inverse, 1)
                    if at == EXP:
                        act.wait_ge(inverse, b * 2 + 1)
                        nc.scalar.activation(ss[:, slot, :, :], ss[:, slot, :, :], ACT.Exp, scale=-0.5).then_inc(inverse, 1)
                    if at == SOFT:
                        act.wait_ge(shifted, b + 1)
                        nc.scalar.activation(s[:, slot, :, :], s[:, slot, :, :], ACT.Exp).then_inc(exped, 1)
                head(0, 0)
                head(0, 1)
                seqs(act, body, finish)

            @block.vector
            def _(dve):
                dve.wait_ge(w_heads, 2)
                nc.vector.tensor_tensor(wl[:, :, :], k.w_kb[:, :, :], wh[:, :, :].bitcast(F32), ALU.subtract).then_inc(w_split, 1)
                nc.vector.tensor_tensor(ql[:, :, :, :], k.qa[:, :, :, :], qh[:, :, :, :].bitcast(F32), ALU.subtract).then_inc(w_split, 1)

                dve.wait_ge(w_split, 2)

                def rest(b, j):
                    x = j % 2
                    dve.wait_ge(headed, b * PAGES + (j + 1))
                    nc.vector.tensor_tensor(cl[:, x, :], xbank[:, 0:2 * P], ch[:, x, :].bitcast(F32), ALU.subtract).then_inc(t_kept, 1)

                def body(b, slot, uses):
                    base = b * PAGES
                    for j in range(PAGES):
                        x = j % 2
                        if j + 2 < PAGES:
                            rest(b, j + 2)
                        elif not is_last(b):
                            rest(b + 1, j + 2 - PAGES)
                        dve.wait_ge(squared, base + (j + 1))
                        nc.vector.tensor_reduce(ss[:, slot, j, :], sq[:, x, :].rearrange("p (h e) -> p h e", e=NOPE), AX.X, ALU.add).then_inc(summed, 1)
                        if j - 1 in ROPE_AT:
                            half = ROPE_AT.index(j - 1)
                            dve.wait_ge(rope_sq, b * 2 + (half + 1))
                            nc.vector.tensor_reduce(ssp[:, 8 * half:8 * half + 8], kpe_sq[:, :, :], AX.X, ALU.add).then_inc(rope_sum, 1)
                        if not is_first(b):
                            finish(b - 1, 1 - slot, j)

                def finish(b, slot, at):
                    if at == TOTAL:
                        dve.wait_ge(summed, b * PAGES + PAGES)
                        dve.wait_ge(rope_sum, b * 2 + 2)
                        nc.vector.tensor_tensor(ss[:, slot, :, :], ss[:, slot, :, :], bc(ssp[:, :], HEADS), ALU.add).then_inc(tot, 1)
                    if at == SCALE:
                        dve.wait_ge(inverse, b * 2 + 2)
                        dve.wait_ge(scored, b * PAGES + PAGES)
                        sv = s[:, slot, 0:PAGES, :].rearrange("p j (h t) -> p (j h) t", t=NS)
                        nc.vector.tensor_tensor(sv, sbank[:, slot, :].rearrange("p (j t) -> p j t", t=NS),
                                                bc(ss[:, slot, :, :].rearrange("p j h -> p (j h)"), NS), ALU.mult)
                        nc.vector.tensor_copy(s[:, slot, PAGES, :], k.new_scores[:, ds(b, 1), :].rearrange("p o c -> p (o c)")).then_inc(scaled, 1)
                    if at == TOP:
                        dve.wait_ge(scaled, b + 1)
                        nc.vector.tensor_reduce(top[:, :], s[:, slot, :, :].rearrange("p j c -> p c j"), AX.X, ALU.max).then_inc(topped, 1)
                    if at == TURN_TOP:
                        dve.wait_ge(top_turned, b + 1)
                        nc.vector.tensor_reduce(peak[:, :], mbank[0:32, 128:256], AX.X, ALU.max).then_inc(step, 1)
                        dve.wait_ge(step, b * 2 + 1)
                        nc.vector.tensor_scalar(diag[:, :], k.col("ident", 0, 32, 32), peak[:, 0:1], None, ALU.mult).then_inc(peaked, 1)
                    if at == SPREAD:
                        dve.wait_ge(spread, b + 1)
                        nc.vector.tensor_tensor(s[:, slot, :, :], s[:, slot, :, :], mbank[:, 256:288].unsqueeze(1).to_broadcast([P, J, 32]), ALU.subtract).then_inc(shifted, 1)
                    if at == PART:
                        dve.wait_ge(exped, b + 1)
                        nc.vector.tensor_reduce(psum_p[:, :], s[:, slot, :, :].rearrange("p j c -> p c j"), AX.X, ALU.add).then_inc(part, 1)
                    if at == VALUES:
                        dve.wait_ge(outed, b + 1)
                        nc.vector.reciprocal(inv[:, :], mbank[:, 64:96]).then_inc(step, 1)
                        dve.wait_ge(step, b * 2 + 2)
                        nc.vector.tensor_tensor(acc[:, :, ds(b, 1), :].rearrange("p r o c -> p r (o c)"), mbank[:, 0:64].rearrange("p (r c) -> p r c", r=2),
                                                inv[:, :].unsqueeze(1).to_broadcast([P, 2, 32]), ALU.mult).then_inc(divided, 1)
                rest(0, 0)
                rest(0, 1)
                seqs(dve, body, finish)
                dve.wait_ge(vmade, 1)
                nc.vector.tensor_copy(k.o_mla[:, :, SEQ:T], mbank[:, 256:512].rearrange("p (h c) -> p h c", h=HEADS))


def rwkv_sample_out(nc, k):
    with Stage(nc) as st:
        stat, stat2 = st.sb("sam_mean", [P, NS]), st.sb("sam_var", [P, NS])
        sq = st.sb("sam_sq", [P, NS, 64])
        rows = st.sb("sam_y_rows", [NSAM, D])
        bank = st.ps("sam_bank", [P, BANK])
        step, sq_ready, v_ready, inverse, normed = (st.sem(n) for n in ("dve_step", "squared", "var_ready", "inverse_root", "normed"))
        out, back, turned = st.sem("y_stored"), st.sem("y_back"), st.sem("y_turned")
        with st.block() as block:
            @block.vector
            def _(dve):
                c = Chain(dve, step)
                y = k.vec_y[:, :, :]
                c(nc.vector.tensor_reduce(stat[:, :], y, AX.X, ALU.add))
                c(nc.vector.tensor_scalar(stat[:, :], stat[:, :], 1.0 / 64, None, ALU.mult))
                c(nc.vector.tensor_tensor(y, y, bc(stat[:, :], 64), ALU.subtract))
                c(nc.vector.tensor_tensor(sq[:, :, :], y, y, ALU.mult))
                nc.vector.tensor_reduce(stat2[:, :], sq[:, :, :], AX.X, ALU.add).then_inc(v_ready, 1)
                dve.wait_ge(inverse, 2)
                nc.vector.tensor_tensor(y, y, bc(stat2[:, :], 64), ALU.mult).then_inc(normed, 1)
                dve.wait_ge(turned, 1)
                for t in range(DT):
                    last = nc.vector.tensor_scalar(k.o_rwkv[:, t, SEQ:T], bank[:, t * NSAM:(t + 1) * NSAM],
                                                   k.par("rwkv_ln_g", t), k.par("rwkv_ln_b", t), ALU.mult, ALU.add)
                c(last)
                c(nc.vector.tensor_tensor(k.o_rwkv[:, :, SEQ:T], k.o_rwkv[:, :, SEQ:T], k.sam_bonus[:, :, :], ALU.add))
                c(nc.vector.tensor_tensor(k.o_rwkv[:, :, SEQ:T], k.o_rwkv[:, :, SEQ:T], k.sam_gate[:, :, :], ALU.mult))

            @block.scalar
            def _(act):
                act.wait_ge(v_ready, 1)
                nc.scalar.activation(stat2[:, :], stat2[:, :], ACT.Ln, bias=k.col("rwkv_eps"), scale=1.0 / 64).then_inc(inverse, 1)
                act.wait_ge(inverse, 1)
                nc.scalar.activation(stat2[:, :], stat2[:, :], ACT.Exp, scale=-0.5).then_inc(inverse, 1)

            @block.sync
            def _(sp):
                sp.wait_ge(normed, 1)
                for b in range(NB):
                    sp.dma_start(k.d["scratch_y"][NS * b:NS * b + NS, :].rearrange("t (h d) -> h t d", d=64),
                                 k.vec_y[16 * b:16 * b + 16, :, :]).then_inc(out, 16)
                sp.wait_ge(out, 16 * NB)
                sp.dma_start(rows[:, :], k.d["scratch_y"]).then_inc(back, 16)

            @block.tensor
            def _(pe):
                pe.wait_ge(back, 16)
                for t in range(DT):
                    last = nc.tensor.transpose(bank[:, t * NSAM:(t + 1) * NSAM], rows[:, t * P:(t + 1) * P], k.col("ident", 0, NSAM, NSAM))
                last.then_inc(turned, 1)


def ssd_project(nc, k):
    G, NZ, NU = 2, 4, 10
    W = 3 + SEQ + NB * (3 + NS)
    w = k.ldram("w_in")
    with Stage(nc) as st:
        ring = st.sb("w_ring", [P, RING, DT * G * P])
        heads, rests = st.sb("w_heads", [P, RING, DT * G * P], F32R), st.sb("w_rests", [P, RING, DT * G * P], F32R)
        raw = st.sb("xbc_padded", [P, RING, G, W])
        acc = st.sb("conv_acc", [P, RING, G, T])
        last_T = st.sb("conv_last", [P, CT, 3 + 3 * NB])
        rows = st.sb("conv_last_rows", [3 + 3 * NB, SSD_CONV_DIM])
        banks = st.ps("ssd_banks", [P, 8, BANK])
        loaded = [st.sem(f"weights_loaded{r}") for r in range(RING)]
        rounded, split = st.sem("weights_rounded"), st.sem("weights_split")
        made, freed, filled, step = (st.sem(n) for n in ("unit_made", "unit_evacuated", "raw_filled", "dve_step"))
        convolved, act_done, kept, zeroed = (st.sem(n) for n in ("tile_convolved", "tile_activated", "last_kept", "pads_zero"))
        turned, rows_kept, stored, dt_made = (st.sem(n) for n in ("rows_turned", "rows_kept", "rows_stored", "dt_made"))
        sample = raw[:, :, :, 3 + SEQ:W].rearrange("p r g (b s) -> p r g b s", s=3 + NS)
        with st.block() as block:
            @block.sync
            def _(sp):
                for u in range(NU + 1):
                    load_unit(sp, k, ring, loaded, split, w, 0, G * P, u // RING, u % RING, u < RING)
                sp.wait_ge(rows_kept, 3)
                sp.dma_start(k.ldram("p_ssm_conv").rearrange("o j c -> (o j) c"), rows[0:3, :]).then_inc(stored, 16)
                sp.dma_start(k.ldram("s_ssm_conv").rearrange("b j c -> (b j) c"), rows[3:3 + 3 * NB, :]).then_inc(stored, 16)
                sp.wait_ge(stored, 32)

            @block.tensor
            def _(pe):
                for u in range(NU):
                    r = u % RING
                    pe.wait_ge(split, u + 1)
                    if u >= RING:
                        pe.wait_ge(freed, u - RING + 1)
                    for g in range(G):
                        for t in range(DT):
                            c = slice((t * G + g) * P, (t * G + g + 1) * P)
                            last = product(nc, banks[:, 2 * r + g, 0:T], heads[:, r, c], rests[:, r, c],
                                           k.hh[:, t, :], k.hl[:, t, :], t == 0, t == DT - 1)
                    last.then_inc(made, 1)
                r = NU % RING
                pe.wait_ge(split, NU + 1)
                for t in range(DT):
                    c = slice(t * G * P, (t * G + 1) * P)
                    last = product(nc, banks[:, 6, 0:T], heads[:, r, c], rests[:, r, c], k.hh[:, t, :], k.hl[:, t, :], t == 0, t == DT - 1)
                last.then_inc(dt_made, 1)
                pe.wait_ge(kept, 2 * (NU - NZ))
                pe.wait_ge(freed, NU)
                for t in range(CT):
                    last = nc.tensor.transpose(banks[0:27, t // 4, t % 4 * P:(t % 4 + 1) * P], last_T[:, t, :], k.col("ident"))
                    if t % 4 == 3:
                        last.then_inc(turned, 1)

            @block.scalar
            def _(act):
                def activate(u):
                    act.wait_ge(convolved, u - NZ + 1)
                    t = 2 * (u - NZ)
                    nc.scalar.activation(k.xbcT[:, t:t + 2, :], acc[:, u % RING, :, :], ACT.Silu).then_inc(act_done, 1)
                def heads_of(u):
                    round_unit(nc, act, ring, heads, loaded, made, rounded, u // RING, u % RING, u < RING)
                heads_of(0)
                for u in range(NU):
                    r = u % RING
                    heads_of(u + 1)
                    act.wait_ge(made, u + 1)
                    src = banks[:, 2 * r:2 * r + 2, :]
                    if u < NZ:
                        nc.scalar.activation(k.zT[:, 2 * u:2 * u + 2, :], src[:, :, 0:T], ACT.Silu).then_inc(freed, 1)
                    else:
                        if u >= NZ + RING:
                            act.wait_ge(convolved, u - NZ - RING + 1)
                        nc.scalar.copy(raw[:, r, :, 3:3 + SEQ], src[:, :, 0:SEQ])
                        nc.scalar.copy(sample[:, r, :, :, 3:3 + NS], src[:, :, SEQ:T].rearrange("p g (b s) -> p g b s", s=NS)).then_inc(freed, 1)
                        if u > NZ:
                            activate(u - 1)
                activate(NU - 1)
                act.wait_ge(dt_made, 1)
                nc.scalar.copy(k.dtT[:, :], banks[0:SSD_HEADS, 6, 0:T])
                for q in range(3):
                    act.wait_ge(turned, q + 1)
                    nc.scalar.copy(rows[:, q * 512:(q + 1) * 512], banks[0:27, q, :]).then_inc(rows_kept, 1)

            @block.vector
            def _(dve):
                c = Chain(dve, step)
                c(nc.vector.memset(raw[:, :, :, 0:3], 0.0))
                rest_unit(nc, dve, ring, heads, rests, rounded, split, 0, 0)
                for u in range(NU):
                    rest_unit(nc, dve, ring, heads, rests, rounded, split, (u + 1) // RING, (u + 1) % RING)
                    if u < NZ:
                        continue
                    r, t0 = u % RING, 2 * (u - NZ)
                    if u >= NZ + RING:
                        dve.wait_ge(act_done, u - NZ - RING + 1)
                    c(nc.vector.tensor_copy(sample[:, r, :, :, 0:3], k.sconv_T[:, t0:t0 + 2, :].rearrange("p g (b j) -> p g b j", j=3)))
                    dve.wait_ge(freed, u + 1)
                    nc.vector.tensor_copy(last_T[:, t0:t0 + 2, 0:3], raw[:, r, :, SEQ:SEQ + 3]).then_inc(kept, 1)
                    nc.vector.tensor_copy(last_T[:, t0:t0 + 2, 3:27].rearrange("p g (b j) -> p g b j", j=3), sample[:, r, :, :, NS:NS + 3]).then_inc(kept, 1)
                    for j in range(4):
                        for g in range(G):
                            tap = k.par("ssd_conv_w", j * CT + t0 + g)
                            op, os = acc[:, r, g, 0:SEQ], acc[:, r, g, SEQ:T].rearrange("p (b s) -> p b s", s=NS)
                            ip, is_ = raw[:, r, g, j:j + SEQ], sample[:, r, g, :, j:j + NS]
                            if j == 0:
                                nc.vector.tensor_scalar(op, ip, tap, k.par("ssd_conv_b", t0 + g), ALU.mult, ALU.add)
                                last = nc.vector.tensor_scalar(os, is_, tap, k.par("ssd_conv_b", t0 + g), ALU.mult, ALU.add)
                            else:
                                nc.vector.scalar_tensor_tensor(op, ip, tap, op, ALU.mult, ALU.add)
                                last = nc.vector.scalar_tensor_tensor(os, is_, tap, os, ALU.mult, ALU.add)
                        if j < 3:
                            c(last)
                        else:
                            last.then_inc(convolved, 1)
                            dve.wait_ge(convolved, u - NZ + 1)


def ssd_tile(nc, k, tile):
    first, R = TOK[tile]
    sam = tile == 2
    cols = slice(first, first + R)
    tri, after = ("segtri", "segtri_after") if sam else ("tri", "tri_after")
    HB = 4 if not sam else 16
    with Stage(nc) as st:
        x_tm, xd, xdd, y = (st.sb(n, [P, D]) for n in ("x_tm", "x_dt", "x_dt_decayed", "y_tm"))
        b_tm = st.sb("b_tm", [P, 2, P])
        M = st.sb("decay_matrix", [P, 16, R])
        cb = st.sb("cb", [P, 2, R])
        dt, da, cs, tmp16 = (st.sb(n, [P, 16]) for n in ("dt", "dt_a", "da_sum", "dt_tmp"))
        a_neg = st.sb("a_neg", [P, 16])
        ecs, edte, etot = (st.sb(n, [P, 16]) for n in ("exp_sum", "exp_to_end", "exp_total"))
        if sam:
            hTs = st.sb("ssm_T", [P, NB, D])
            Cm = st.sb("c_by_seq", [P, 2, NB, NSAM])
            Bm = st.sb("b_by_seq", [NSAM, 2, NB, P])
            da_rep = st.sb("da_rep", [NSAM, D])
            dec = st.sb("state_decay", [P, DT, NB])
        banks = st.ps("ssdt_banks", [P, 8, BANK])
        step, dt_turned, x_turned, x_kept, b_kept = (st.sem(n) for n in ("dve_step", "dt_turned", "x_turned", "x_kept", "b_kept"))
        abs_in, abs_out, soft, da_ready, a_ready = (st.sem(n) for n in ("dt_biased", "dt_abs", "softplus_log", "da_ready", "a_ready"))
        sums, rows_made, cb_made = (st.sem(n) for n in ("sums_made", "decay_rows_made", "cb_made"))
        m_arg, m_exp, m_ready, e_ready = (st.sem(n) for n in ("decay_argument", "decay_exp", "decay_ready", "exps_ready"))
        xdd_ready, yd_made, yo_made, s_made = (st.sem(n) for n in ("x_decayed_ready", "y_inside_made", "y_state_made", "state_made"))
        y_ready, y_turned, h_ready = (st.sem(n) for n in ("y_ready", "y_turned", "state_ready"))
        h_turned, h_kept, h_out = (st.sem(n) for n in ("state_turned", "state_kept", "state_stored"))
        state_in = st.sem("ssm_state_loaded")
        cm_ready, bm_ready, dec_made, dec_ready = (st.sem(n) for n in ("c_masked", "b_masked", "decay_sums", "decay_native"))
        with st.block() as block:
            @block.tensor
            def _(pe):
                ident = k.col("ident")
                nc.tensor.transpose(banks[0:R, 3, 0:16], k.dtT[:, cols], k.col("ident", 0, 16, 16)).then_inc(dt_turned, 1)
                for t in range(DT):
                    last = nc.tensor.transpose(banks[0:R, 1 + t // 4, t % 4 * P:(t % 4 + 1) * P], k.xbcT[:, t, cols], ident)
                last.then_inc(x_turned, 1)
                for g in range(2):
                    last = nc.tensor.transpose(banks[0:R, 0, 32 + g * P:32 + (g + 1) * P], k.xbcT[:, 8 + g, cols], ident)
                last.then_inc(x_turned, 1)
                for g in range(2):
                    last = nc.tensor.matmul(banks[0:R, 7, g * R:(g + 1) * R], k.xbcT[:, 8 + g, cols], k.xbcT[:, 10 + g, cols],
                                            start=True, stop=True, skip_group_check=True)
                last.then_inc(cb_made, 1)
                pe.wait_ge(da_ready, 1)
                pe.wait_ge(b_kept, 1)
                nc.tensor.matmul(banks[0:R, 0, 288:304], k.col(tri, rows=R), da[0:R, :], start=True, stop=True, skip_group_check=True)
                nc.tensor.matmul(banks[0:R, 0, 304:320], k.col(after, rows=R), da[0:R, :], start=True, stop=True, skip_group_check=True)
                nc.tensor.matmul(banks[:, 0, 320:336], k.const[0:R, CCOL["ones"][0]:CCOL["ones"][0] + P], da[0:R, :],
                                 start=True, stop=True, skip_group_check=True).then_inc(sums, 1)
                for h in range(16):
                    last = nc.tensor.matmul(banks[0:R, 3 + h // HB, h % HB * R:(h % HB + 1) * R], da[0:R, h:h + 1].to_broadcast([R, R]),
                                            k.col(tri, rows=R), start=True, stop=True, skip_group_check=True)
                    if h % HB == HB - 1:
                        last.then_inc(rows_made, 1)
                if sam:
                    for q in range(16):
                        b, half = q // 2, q % 2
                        if q >= 2:
                            pe.wait_ge(h_kept, q - 1)
                        for i in range(4):
                            last = nc.tensor.transpose(banks[:, 5 + q % 2, i * P:(i + 1) * P], k.ssm_nat[:, b, 4 * half + i, :], ident)
                        last.then_inc(h_turned, 1)
                    pe.wait_ge(h_kept, 16)
                    pe.wait_ge(cm_ready, 1)
                pe.wait_ge(m_ready, 1)
                pe.wait_ge(x_kept, 1)
                for h in range(16):
                    last = nc.tensor.matmul(banks[0:R, 1 + h // 8, h % 8 * 64:(h % 8 + 1) * 64], M[0:R, h, :], xd[0:R, h * 64:(h + 1) * 64],
                                            start=True, stop=True, skip_group_check=True)
                last.then_inc(yd_made, 1)
                for g in range(2):
                    if not sam:
                        last = nc.tensor.matmul(banks[:, 3 + g, :], k.xbcT[:, 10 + g, cols], k.ssm_T[:, g * 512:(g + 1) * 512], start=True, stop=True)
                    else:
                        for b in range(NB):
                            last = nc.tensor.matmul(banks[0:R, 3 + g, :], Cm[:, g, b, :], hTs[:, b, g * 512:(g + 1) * 512], start=b == 0, stop=b == NB - 1)
                last.then_inc(yo_made, 1)
                pe.wait_ge(xdd_ready, 1)
                if not sam:
                    for g in range(2):
                        last = nc.tensor.matmul(banks[:, 5 + g, :], b_tm[:, g, :], xdd[:, g * 512:(g + 1) * 512], start=True, stop=True)
                    last.then_inc(s_made, 1)
                else:
                    pe.wait_ge(bm_ready, 1)
                    for t in range(DT):
                        last = nc.tensor.matmul(banks[:, 7, 64 + t * NB:64 + (t + 1) * NB], da_rep[:, t * P:(t + 1) * P], k.col("seg", rows=NSAM),
                                               start=True, stop=True, skip_group_check=True)
                    last.then_inc(dec_made, 1)
                    for t in range(DT):
                        if t:
                            pe.wait_ge(h_ready, t)
                        for half in range(2):
                            last = nc.tensor.matmul(banks[:, 5 + half, :], xdd[0:R, t * P:(t + 1) * P],
                                                    Bm[:, t // 4, 4 * half:4 * half + 4, :].rearrange("p b n -> p (b n)"), start=True, stop=True)
                        last.then_inc(s_made, 1)
                pe.wait_ge(y_ready, 1)
                for t in range(DT):
                    last = nc.tensor.transpose(banks[:, 3 + t // 4, t % 4 * R:(t % 4 + 1) * R], y[0:R, t * P:(t + 1) * P], k.col("ident", 0, R, R))
                last.then_inc(y_turned, 1)
                if tile == 1:
                    pe.wait_ge(h_ready, 1)
                    for t in range(DT):
                        last = nc.tensor.transpose(banks[:, 1 + t // 4, t % 4 * P:(t % 4 + 1) * P], k.ssm_T[:, t * P:(t + 1) * P], ident)
                    last.then_inc(h_turned, 1)

            @block.scalar
            def _(act):
                nc.scalar.activation(a_neg[:, :], k.a_log[:, :], ACT.Exp).then_inc(a_ready, 1)
                act.wait_ge(abs_in, 1)
                nc.scalar.activation(tmp16[0:R, :], dt[0:R, :], ACT.Abs).then_inc(abs_out, 1)
                act.wait_ge(abs_out, 1)
                nc.scalar.activation(tmp16[0:R, :], tmp16[0:R, :], ACT.Exp, scale=-1.0).then_inc(abs_out, 1)
                act.wait_ge(abs_out, 2)
                nc.scalar.activation(tmp16[0:R, :], tmp16[0:R, :], ACT.Ln, bias=k.col("ones", 0, 1, R)).then_inc(soft, 1)
                act.wait_ge(x_turned, 2)
                nc.scalar.copy(x_tm[0:R, :], banks[0:R, 1:3, :]).then_inc(x_kept, 1)
                nc.scalar.copy(b_tm[0:R, :, :], banks[0:R, 0, 32:288]).then_inc(b_kept, 1)
                act.wait_ge(sums, 1)
                nc.scalar.activation(ecs[0:R, :], banks[0:R, 0, 288:304], ACT.Exp)
                nc.scalar.activation(edte[0:R, :], banks[0:R, 0, 304:320], ACT.Exp)
                nc.scalar.activation(etot[:, :], banks[:, 0, 320:336], ACT.Exp).then_inc(e_ready, 1)
                act.wait_ge(m_arg, 1)
                nc.scalar.activation(M[0:R, :, :], M[0:R, :, :], ACT.Exp).then_inc(m_exp, 1)
                if sam:
                    for q in range(16):
                        act.wait_ge(h_turned, q + 1)
                        nc.scalar.copy(hTs[:, q // 2, q % 2 * 512:(q % 2 + 1) * 512], banks[:, 5 + q % 2, :]).then_inc(h_kept, 1)
                    act.wait_ge(dec_made, 1)
                    nc.scalar.activation(dec[:, :, :], banks[:, 7, 64:128], ACT.Exp).then_inc(dec_ready, 1)
                if tile == 1:
                    act.wait_ge(h_turned, 1)
                    nc.scalar.copy(xd[:, :], banks[:, 1:3, :]).then_inc(h_kept, 1)

            @block.vector
            def _(dve):
                c = Chain(dve, step)
                r16 = slice(0, R)
                dve.wait_ge(dt_turned, 1)
                nc.vector.tensor_tensor(dt[r16, :], banks[0:R, 3, 0:16], k.dt_bias[r16, :], ALU.add).then_inc(abs_in, 1)
                dve.wait_ge(a_ready, 1)
                c(nc.vector.tensor_scalar(a_neg[:, :], a_neg[:, :], -1.0, None, ALU.mult))
                dve.wait_ge(soft, 1)
                c(nc.vector.scalar_tensor_tensor(dt[r16, :], dt[r16, :], 0.0, tmp16[r16, :], ALU.max, ALU.add))
                nc.vector.tensor_tensor(da[r16, :], dt[r16, :], a_neg[r16, :], ALU.mult).then_inc(da_ready, 1)
                dve.wait_ge(da_ready, 1)
                if sam:
                    c(nc.vector.tensor_copy(da_rep[:, :].rearrange("p (h d) -> p h d", d=64), bc(da[r16, :], 64)))
                xh, xdh, xddh, yh = (b[r16, :].rearrange("p (h d) -> p h d", d=64) for b in (x_tm, xd, xdd, y))
                dve.wait_ge(cb_made, 1)
                c(nc.vector.tensor_tensor(cb[r16, :, :], banks[0:R, 7, 0:2 * R].rearrange("p (g l) -> p g l", g=2),
                                          k.col(tri, rows=R).unsqueeze(1).to_broadcast([R, 2, R]), ALU.mult))
                dve.wait_ge(e_ready, 1)
                c(nc.vector.tensor_copy(cs[r16, :], banks[0:R, 0, 288:304]))
                for q in range(16 // HB):
                    dve.wait_ge(rows_made, q + 1)
                    last = nc.vector.tensor_tensor(M[r16, q * HB:(q + 1) * HB, :], banks[0:R, 3 + q, 0:HB * R].rearrange("p (h l) -> p h l", h=HB),
                                                   bc(cs[r16, q * HB:(q + 1) * HB], R), ALU.subtract)
                c(last)
                nc.vector.tensor_scalar(M[r16, :, :], M[r16, :, :], 0.0, None, ALU.min).then_inc(m_arg, 1)
                dve.wait_ge(x_kept, 1)
                c(nc.vector.tensor_tensor(xdh, xh, bc(dt[r16, :], 64), ALU.mult))
                dve.wait_ge(m_exp, 1)
                for g in range(2):
                    last = nc.vector.tensor_tensor(M[r16, 8 * g:8 * g + 8, :], M[r16, 8 * g:8 * g + 8, :],
                                                   cb[r16, g:g + 1, :].to_broadcast([R, 8, R]), ALU.mult)
                last.then_inc(m_ready, 1)
                if sam:
                    c(nc.vector.memset(Cm[:, :, :, :], 0.0))
                    for g in range(2):
                        for b in range(NB):
                            last = nc.vector.tensor_copy(Cm[:, g, b, b * NS:(b + 1) * NS], k.xbcT[:, 10 + g, first + b * NS:first + (b + 1) * NS])
                    last.then_inc(cm_ready, 1)
                    dve.wait_ge(b_kept, 1)
                    for g in range(2):
                        last = nc.vector.tensor_tensor(Bm[:, g, :, :], b_tm[r16, g:g + 1, :].to_broadcast([R, NB, P]),
                                                       bc(k.col("seg", rows=NSAM), P), ALU.mult)
                    last.then_inc(bm_ready, 1)
                dve.wait_ge(e_ready, 1)
                nc.vector.tensor_tensor(xddh, xdh, bc(edte[r16, :], 64), ALU.mult).then_inc(xdd_ready, 1)
                c(nc.vector.tensor_tensor(xh, xh, bc(k.ssd_d[r16, :], 64), ALU.mult))
                dve.wait_ge(yo_made, 1)
                for g in range(2):
                    last = nc.vector.tensor_tensor(yh[:, 8 * g:8 * g + 8, :], banks[0:R, 3 + g, :].rearrange("p (h d) -> p h d", d=64),
                                                   bc(ecs[r16, 8 * g:8 * g + 8], 64), ALU.mult)
                c(last)
                c(nc.vector.tensor_tensor(y[r16, :], y[r16, :], banks[0:R, 1:3, :].rearrange("p a n -> p (a n)"), ALU.add))
                nc.vector.tensor_tensor(y[r16, :], y[r16, :], x_tm[r16, :], ALU.add).then_inc(y_ready, 1)
                if not sam:
                    dve.wait_ge(s_made, 1)
                    hv = k.ssm_T[:, :].rearrange("p (h d) -> p h d", d=64)
                    c(nc.vector.tensor_tensor(hv, hv, bc(etot[:, :], 64), ALU.mult))
                    nc.vector.tensor_tensor(k.ssm_T[:, :], k.ssm_T[:, :], banks[:, 5:7, :].rearrange("p a n -> p (a n)"), ALU.add).then_inc(h_ready, 1)
                else:
                    dve.wait_ge(dec_ready, 1)
                    for t in range(DT):
                        c(nc.vector.tensor_tensor(k.ssm_nat[:, :, t, :], k.ssm_nat[:, :, t, :], bc(dec[:, t, :], P), ALU.mult))
                        dve.wait_ge(s_made, t + 1)
                        nc.vector.tensor_tensor(k.ssm_nat[:, :, t, :], banks[:, 5:7, :].rearrange("p a (b n) -> p (a b) n", n=P),
                                                k.ssm_nat[:, :, t, :], ALU.add).then_inc(h_ready, 1)
                dve.wait_ge(y_turned, 1)
                for half in range(2):
                    last = nc.vector.tensor_tensor(k.yT[:, 4 * half:4 * half + 4, cols], banks[:, 3 + half, 0:4 * R].rearrange("p (t r) -> p t r", t=4),
                                                   k.zT[:, 4 * half:4 * half + 4, cols], ALU.mult)
                c(last)

            @block.sync
            def _(sp):
                if tile == 0:
                    for b in range(NB):
                        sp.dma_start(k.ssm_nat[:, b, :, :], k.ldram("state_ssm")[b:b + 1].rearrange("b (t h) p n -> (b h p) t n", h=2)).then_inc(state_in, 16)
                    sp.wait_ge(state_in, 16 * NB)
                elif sam:
                    sp.wait_ge(h_ready, DT)
                    for b in range(NB):
                        sp.dma_start(k.ldram("s_ssm")[b:b + 1].rearrange("b (t h) p n -> (b h p) t n", h=2), k.ssm_nat[:, b, :, :]).then_inc(h_out, 16)
                    sp.wait_ge(h_out, 16 * NB)
                else:
                    sp.wait_ge(h_kept, 1)
                    sp.dma_start(k.ldram("p_ssm").rearrange("o (t h) p n -> (o h p) t n", h=2), xd[:, :].rearrange("p (t n) -> p t n", n=P)).then_inc(h_out, 16)
                    sp.wait_ge(h_out, 16)


def ssd_norm(nc, k):
    with Stage(nc) as st:
        sq = st.sb("ssd_sq", [P, DT, T])
        inv = st.sb("ssd_inv", [P, 2, T])
        banks = st.ps("ssd_sum", [P, 2, BANK])
        squared, summed, inverse = st.sem("squared"), st.sem("summed"), st.sem("inverse_root")
        with st.block() as block:
            @block.scalar
            def _(act):
                for g in range(2):
                    nc.scalar.activation(sq[:, 4 * g:4 * g + 4, :], k.yT[:, 4 * g:4 * g + 4, :], ACT.Square).then_inc(squared, 1)
                for g in range(2):
                    act.wait_ge(summed, g + 1)
                    nc.scalar.activation(inv[:, g, :], banks[:, g, 0:T], ACT.Ln, bias=k.col("eps"), scale=1.0 / 512).then_inc(inverse, 1)
                act.wait_ge(inverse, 2)
                nc.scalar.activation(inv[:, :, :], inv[:, :, :], ACT.Exp, scale=-0.5).then_inc(inverse, 1)

            @block.tensor
            def _(pe):
                for g in range(2):
                    pe.wait_ge(squared, g + 1)
                    for t in range(4):
                        last = nc.tensor.matmul(banks[:, g, 0:T], k.col("ones"), sq[:, 4 * g + t, :], start=t == 0, stop=t == 3)
                    last.then_inc(summed, 1)

            @block.vector
            def _(dve):
                dve.wait_ge(inverse, 3)
                for d in range(DT):
                    nc.vector.scalar_tensor_tensor(k.yT[:, d, :], k.yT[:, d, :], k.par("ssd_norm_g", d), inv[:, d // 4, :], ALU.mult, ALU.mult)


def merge(nc, k):
    N = 3 * DT
    NU = N + DT // 2
    wg = k.ldram("w_gate")
    with Stage(nc) as st:
        ring = st.sb("w_ring", [P, RING, 2 * DT * P])
        heads, rests = st.sb("w_heads", [P, RING, 2 * DT * P], F32R), st.sb("w_rests", [P, RING, 2 * DT * P], F32R)
        oh, ol = st.sb("out_heads", [P, 2, DT, T], F32R), st.sb("out_rests", [P, 2, DT, T], F32R)
        gate, term = st.sb("gate", [P, 2, T]), st.sb("gated", [P, T])
        merged = st.sb("merged", [P, DT, T])
        banks = st.ps("merge_banks", [P, 8, BANK])
        loaded = [st.sem(f"weights_loaded{r}") for r in range(RING)]
        rounded, split, out_rounded, out_split = (st.sem(n) for n in ("weights_rounded", "weights_split", "outputs_rounded", "outputs_split"))
        made, gated, joined, step = (st.sem(n) for n in ("unit_made", "gate_ready", "unit_joined", "dve_step"))
        branches = (("w_o_ssd", k.yT), ("w_o_rwkv", k.o_rwkv), ("w_o_mla", k.o_mla))
        SPLIT_AT = {0: 0, 2: 1, DT + 1: 2}
        with st.block() as block:
            @block.sync
            def _(sp):
                for u in range(NU):
                    r = u % RING
                    if u >= RING:
                        sp.wait_ge(split, u - RING + 1)
                    for g in range(2):
                        if u < N:
                            br, d = u // DT, u % DT
                            src = wg[:, u * P:(u + 1) * P] if g == 0 else k.ldram(branches[br][0])[:, d * P:(d + 1) * P]
                        else:
                            d = 2 * (u - N) + g
                            src = k.ldram("w_out")[:, d * P:(d + 1) * P]
                        sp.dma_start(ring[:, r, g * DT * P:(g + 1) * DT * P].rearrange("p (t n) -> p t n", n=P),
                                     src.rearrange("(t p) n -> p t n", p=P)).then_inc(loaded[r], 16)

            @block.tensor
            def _(pe):
                for u in range(NU):
                    r, br = u % RING, u // DT
                    pe.wait_ge(split, u + 1)
                    if u >= 4:
                        pe.wait_ge(joined, u - 3)
                    for g in range(2):
                        if g == 0 and u < N:
                            xh, xl = k.hh, k.hl
                        else:
                            if u % DT == 0:
                                pe.wait_ge(out_split, br + 1 if br < 3 else 3 + DT)
                            xh, xl = oh[:, br % 2, :, :], ol[:, br % 2, :, :]
                        for t in range(DT):
                            c = slice((g * DT + t) * P, (g * DT + t + 1) * P)
                            last = product(nc, banks[:, 2 * (u % 4) + g, 0:T], heads[:, r, c], rests[:, r, c],
                                           xh[:, t, :], xl[:, t, :], t == 0, t == DT - 1)
                    last.then_inc(made, 1)

            @block.scalar
            def _(act):
                def heads_of(u):
                    if u < NU:
                        round_unit(nc, act, ring, heads, loaded, made, rounded, u // RING, u % RING, u < RING, per=32)
                heads_of(0)
                for u in range(N):
                    if u in SPLIT_AT:
                        br = SPLIT_AT[u]
                        if br == 2:
                            act.wait_ge(made, DT)
                        nc.scalar.copy(oh[:, br % 2, :, :], branches[br][1][:, :, :]).then_inc(out_rounded, 1)
                    heads_of(u + 1)
                    act.wait_ge(made, u + 1)
                    if u >= 2:
                        act.wait_ge(joined, u - 1)
                    nc.scalar.activation(gate[:, u % 2, :], banks[:, 2 * (u % 4), 0:T], ACT.Sigmoid, bias=k.par("b_gate", u)).then_inc(gated, 1)
                    if u >= 2 * DT + 1:
                        act.wait_ge(joined, u)
                        nc.scalar.copy(oh[:, 1, u - 1 - 2 * DT, :], merged[:, u - 1 - 2 * DT, :]).then_inc(out_rounded, 1)
                act.wait_ge(joined, N)
                nc.scalar.copy(oh[:, 1, DT - 1, :], merged[:, DT - 1, :]).then_inc(out_rounded, 1)
                for u in range(N + 1, NU):
                    heads_of(u)

            @block.vector
            def _(dve):
                c = Chain(dve, step)

                def rests_of(u):
                    if u < NU:
                        rest_unit(nc, dve, ring, heads, rests, rounded, split, u // RING, u % RING)

                def merged_rest(d):
                    dve.wait_ge(out_rounded, 3 + d + 1)
                    nc.vector.tensor_tensor(ol[:, 1, d, :], merged[:, d, :], oh[:, 1, d, :].bitcast(F32), ALU.subtract).then_inc(out_split, 1)
                rests_of(0)
                for u in range(N):
                    d = u % DT
                    if u in SPLIT_AT:
                        br = SPLIT_AT[u]
                        dve.wait_ge(out_rounded, br + 1)
                        nc.vector.tensor_tensor(ol[:, br % 2, :, :], branches[br][1][:, :, :], oh[:, br % 2, :, :].bitcast(F32), ALU.subtract).then_inc(out_split, 1)
                    rests_of(u + 1)
                    if u >= 2 * DT + 2:
                        merged_rest(u - 2 - 2 * DT)
                    dve.wait_ge(gated, u + 1)
                    ps = banks[:, 2 * (u % 4) + 1, 0:T]
                    if u < DT:
                        nc.vector.tensor_tensor(merged[:, d, :], ps, gate[:, u % 2, :], ALU.mult).then_inc(joined, 1)
                    else:
                        c(nc.vector.tensor_tensor(term[:, :], ps, gate[:, u % 2, :], ALU.mult))
                        nc.vector.tensor_tensor(merged[:, d, :], merged[:, d, :], term[:, :], ALU.add).then_inc(joined, 1)
                        dve.wait_ge(joined, u + 1)
                for d in (DT - 2, DT - 1):
                    merged_rest(d)
                for u in range(N, NU):
                    rests_of(u + 1)
                    dve.wait_ge(made, u + 1)
                    d = 2 * (u - N)
                    nc.vector.tensor_tensor(k.xT[:, d:d + 2, :], banks[:, 2 * (u % 4):2 * (u % 4) + 2, 0:T], k.xT[:, d:d + 2, :], ALU.add).then_inc(joined, 1)


def ffn(nc, k):
    W = 2 + SEQ + NB * (2 + NS)
    HT, ND = FT // 2, 2 * DT
    wu = k.ldram("ffn_w_up")
    with Stage(nc) as st:
        ring = st.sb("w_ring", [P, RING, 2 * DT * P])
        heads, rests = st.sb("w_heads", [P, RING, 2 * DT * P], F32R), st.sb("w_rests", [P, RING, 2 * DT * P], F32R)
        raw = st.sb("up_padded", [P, RING, 2, W])
        acc = st.sb("conv_acc", [P, RING, 2, T])
        gate = st.sb("up_silu", [P, RING, T])
        prod = st.sb("ffn_product", [P, RING, T])
        ah, al = st.sb("ffn_act_heads", [P, FT, T], F32R), st.sb("ffn_act_rests", [P, FT, T], F32R)
        last_T = st.sb("conv_last", [P, 2 * FT, 2 + 2 * NB])
        rows = st.sb("conv_last_rows", [2 + 2 * NB, 3, BANK])
        banks = st.ps("ffn_banks", [P, 8, BANK])
        loaded = [st.sem(f"weights_loaded{r}") for r in range(RING)]
        rounded, split, act_rounded, act_split = (st.sem(n) for n in ("weights_rounded", "weights_split", "product_rounded", "product_split"))
        split_pool = st.sem("second_half_split")
        made, freed, convolved, silu_done, unit_done = (st.sem(n) for n in ("unit_made", "unit_evacuated", "unit_convolved", "silu_ready", "unit_done"))
        step, kept, turned, rows_kept = (st.sem(n) for n in ("dve_step", "pads_zero", "rows_turned", "rows_kept"))
        stored = [st.sem(f"rows_stored{r}") for r in range(3)]
        added = st.sem("x_added")
        sample = raw[:, :, :, 2 + SEQ:W].rearrange("p r g (b s) -> p r g b s", s=2 + NS)
        with st.block() as block:
            @block.sync
            def _(sp):
                def unit(i, r, first):
                    if not first:
                        sp.wait_ge(split, (i - 1) * RING + r + 1)
                        sp.wait_ge(split_pool, (i - 1) * RING + r + 1)
                    for g in range(2):
                        sp.dma_start(ring[:, r, g * DT * P:(g + 1) * DT * P].rearrange("p (t n) -> p t n", n=P),
                                     wu[:, ds((i * RING + r) * P + g * D_FF, P)].rearrange("(t p) n -> p t n", p=P)).then_inc(loaded[r], 16)
                rounds(sp, FT, RING, unit)
                for u in range(FT, FT + ND):
                    r, d, half = u % RING, (u - FT) // 2, (u - FT) % 2
                    sp.wait_ge(split, u - RING + 1)
                    sp.wait_ge(split_pool, min(u - RING + 1, FT))
                    for q, (t0, t1) in enumerate(((0, 6), (6, HT))):
                        sp.dma_start(ring[:, r, t0 * P:t1 * P].rearrange("p (t n) -> p t n", n=P),
                                     k.ldram("ffn_w_down")[(half * HT + t0) * P:(half * HT + t1) * P, d * P:(d + 1) * P].rearrange(
                                         "(t p) n -> p t n", p=P)).then_inc(loaded[r], 16)

            @block.gpsimd
            def _(pool):
                def unit(i, r, first):
                    pool.wait_ge(rounded, i * RING + (r + 1))
                    c = slice(DT * P, 2 * DT * P)
                    nc.gpsimd.tensor_tensor(rests[:, r, c], ring[:, r, c], heads[:, r, c].bitcast(F32), ALU.subtract).then_inc(split_pool, 1)
                rounds(pool, FT, RING, unit)

            @block.tensor
            def _(pe):
                def unit(i, r, first):
                    pe.wait_ge(split, i * RING + (r + 1))
                    pe.wait_ge(split_pool, i * RING + (r + 1))
                    if not first:
                        pe.wait_ge(freed, (i - 1) * RING + r + 1)
                    for g in range(2):
                        for t in range(DT):
                            c = slice((g * DT + t) * P, (g * DT + t + 1) * P)
                            last = product(nc, banks[:, 2 * r + g, 0:T], heads[:, r, c], rests[:, r, c],
                                           k.hh[:, t, :], k.hl[:, t, :], t == 0, t == DT - 1)
                    last.then_inc(made, 1)
                rounds(pe, FT, RING, unit)
                for u in range(FT, FT + ND):
                    r, d, half = u % RING, (u - FT) // 2, (u - FT) % 2
                    if d == 0:
                        pe.wait_ge(act_split, FT if half else HT)
                    pe.wait_ge(split, u + 1)
                    if d >= 2 and half == 0:
                        pe.wait_ge(added, d - 1)
                    for t in range(HT):
                        c = slice(t * P, (t + 1) * P)
                        last = product(nc, banks[:, 6 + d % 2, 0:T], heads[:, r, c], rests[:, r, c], ah[:, half * HT + t, :],
                                       al[:, half * HT + t, :], half == 0 and t == 0, half == 1 and t == HT - 1)
                    last.then_inc(made, 1)
                    if 1 <= u - FT < 12:
                        q = u - FT - 1
                        pe.wait_ge(freed, FT)
                        if q >= 6:
                            pe.wait_ge(rows_kept, q - 5)
                        for i in range(4):
                            last = nc.tensor.transpose(banks[0:18, q % 6, i * P:(i + 1) * P], last_T[:, 4 * q + i, :], k.col("ident"))
                        last.then_inc(turned, 1)

            @block.scalar
            def _(act):
                def silu(u, r):
                    act.wait_ge(convolved, u + 1)
                    nc.scalar.activation(gate[:, r, :], acc[:, r, 0, :], ACT.Silu).then_inc(silu_done, 1)

                def round_product(u, r):
                    act.wait_ge(unit_done, u + 1)
                    nc.scalar.copy(ah[:, ds(u, 1), :].rearrange("p o t -> p (o t)"), prod[:, r, :]).then_inc(act_rounded, 1)

                def heads_of(i, r, first, tiles=2 * DT):
                    round_unit(nc, act, ring, heads, loaded, made, rounded, i, r, first, per=32, tiles=tiles)
                heads_of(0, 0, True)

                def unit(i, r, first):
                    u = i * RING + r
                    if isinstance(i, int) and u == FT - 1:
                        heads_of(*following(i, r), tiles=HT)
                    else:
                        heads_of(*following(i, r))
                    act.wait_ge(made, u + 1)
                    if not first:
                        act.wait_ge(convolved, (i - 1) * RING + r + 1)
                    src = banks[:, 2 * r:2 * r + 2, :]
                    nc.scalar.copy(raw[:, r, :, 2:2 + SEQ], src[:, :, 0:SEQ])
                    nc.scalar.copy(sample[:, r, :, :, 2:2 + NS], src[:, :, SEQ:T].rearrange("p g (b s) -> p g b s", s=NS)).then_inc(freed, 1)
                    if not (first and r == 0):
                        if not first:
                            act.wait_ge(unit_done, (i - 1) * RING + r)
                        silu(u - 1, (r - 1) % RING)
                    if not (first and r < 2):
                        round_product(u - 2, (r - 2) % RING)
                rounds(act, FT, RING, unit)
                silu(FT - 1, (FT - 1) % RING)
                for u in (FT - 2, FT - 1):
                    round_product(u, u % RING)
                for u in range(FT, FT + ND):
                    if u + 1 < FT + ND:
                        heads_of((u + 1) // RING, (u + 1) % RING, False, tiles=HT)
                    q = u - FT - 1
                    if 0 <= q < 11:
                        act.wait_ge(turned, q + 1)
                        if q >= 3:
                            act.wait_ge(stored[q % 3], 32 * (q // 3))
                        nc.scalar.copy(rows[:, q % 3, :], banks[0:18, q % 6, :]).then_inc(rows_kept, 1)
                        act.wait_ge(rows_kept, q + 1)
                        c = slice(q * BANK, (q + 1) * BANK)
                        act.dma_start(k.ldram("p_ffn_conv").rearrange("o j c -> (o j) c")[:, c], rows[0:2, q % 3, :]).then_inc(stored[q % 3], 16)
                        act.dma_start(k.ldram("s_ffn_conv").rearrange("b j c -> (b j) c")[:, c], rows[2:2 + 2 * NB, q % 3, :]).then_inc(stored[q % 3], 16)
                for r in range(3):
                    act.wait_ge(stored[r], 32 * len(range(r, 11, 3)))

            @block.vector
            def _(dve):
                nc.vector.memset(raw[:, :, :, 0:2], 0.0).then_inc(kept, 1)
                dve.wait_ge(kept, 1)
                PER = 3

                def rests_of(i, r, tiles=DT):
                    rest_unit(nc, dve, ring, heads, rests, rounded, split, i, r, tiles=tiles)
                rests_of(0, 0)

                def product_rest(u, r):
                    dve.wait_ge(act_rounded, u + 1)
                    one = (slice(None), ds(u, 1), slice(None))
                    nc.vector.tensor_tensor(al[one].rearrange("p o t -> p (o t)"), prod[:, r, :],
                                            ah[one].bitcast(F32).rearrange("p o t -> p (o t)"), ALU.subtract).then_inc(act_split, 1)

                def finish(u, r):
                    dve.wait_ge(silu_done, u + 1)
                    nc.vector.tensor_tensor(prod[:, r, :], gate[:, r, :], acc[:, r, 1, :], ALU.mult).then_inc(unit_done, 1)

                def unit(i, r, first):
                    u = i * RING + r
                    last_unit = isinstance(i, int) and u == FT - 1
                    rests_of(*following(i, r)[0:2], tiles=HT if last_unit else DT)
                    if not first:
                        dve.wait_ge(unit_done, (i - 1) * RING + r + 1)
                    c = Chain(dve, step, u * PER)
                    pad = [sample[:, r, g, :, 0:2] for g in range(2)]
                    for g in range(2):
                        last = nc.vector.tensor_copy(pad[g], k.fconv_T[:, ds(u + g * FT, 1), :].rearrange("p o (b j) -> p (o b) j", j=2))
                    c(last)
                    dve.wait_ge(freed, u + 1)
                    for g in range(2):
                        nc.vector.tensor_copy(last_T[:, ds(u + g * FT, 1), 0:2].rearrange("p o c -> p (o c)"), raw[:, r, g, SEQ:SEQ + 2])
                        nc.vector.tensor_copy(last_T[:, ds(u + g * FT, 1), 2:18].rearrange("p o (b j) -> p (o b) j", j=2), sample[:, r, g, :, NS:NS + 2])
                    for j in range(3):
                        for g in range(2):
                            at = PCOL["ffn_conv_w01"][0] + j * 2 * FT if j < 2 else PCOL["ffn_conv_w2"][0]
                            tap = k.params[:, ds(u + (at + g * FT), 1)]
                            bias = k.params[:, ds(u + (PCOL["ffn_conv_b"][0] + g * FT), 1)]
                            op, os = acc[:, r, g, 0:SEQ], acc[:, r, g, SEQ:T].rearrange("p (b s) -> p b s", s=NS)
                            ip, is_ = raw[:, r, g, j:j + SEQ], sample[:, r, g, :, j:j + NS]
                            if j == 0:
                                nc.vector.tensor_scalar(op, ip, tap, bias, ALU.mult, ALU.add)
                                last = nc.vector.tensor_scalar(os, is_, tap, bias, ALU.mult, ALU.add)
                            else:
                                nc.vector.scalar_tensor_tensor(op, ip, tap, op, ALU.mult, ALU.add)
                                last = nc.vector.scalar_tensor_tensor(os, is_, tap, os, ALU.mult, ALU.add)
                        if j < 2:
                            c(last)
                        else:
                            last.then_inc(convolved, 1)
                            dve.wait_ge(convolved, u + 1)
                    if not (first and r == 0):
                        if not (first and r < 3):
                            product_rest(u - 3, r)
                        finish(u - 1, (r - 1) % RING)
                rounds(dve, FT, RING, unit)
                dve.wait_ge(act_split, FT - 3)
                finish(FT - 1, (FT - 1) % RING)
                for u in (FT - 3, FT - 2, FT - 1):
                    product_rest(u, u % RING)
                for d in range(DT):
                    for u in (FT + 2 * d + 1, FT + 2 * d + 2):
                        if u < FT + ND:
                            rests_of(u // RING, u % RING, tiles=HT)
                    dve.wait_ge(made, FT + 2 * d + 2)
                    nc.vector.tensor_tensor(k.xT[:, d, :], banks[:, 6 + d % 2, 0:T], k.xT[:, d, :], ALU.add).then_inc(added, 1)


def store_x(nc, k):
    with Stage(nc) as st:
        x_tm = st.sb("x_tm", [P, 3, D])
        banks = st.ps("x_banks", [P, 6, BANK])
        turned, kept, stored = st.sem("x_turned"), st.sem("x_rows_ready"), st.sem("x_stored")
        with st.block() as block:
            @block.tensor
            def _(pe):
                for n, (first, rows) in enumerate(TOK):
                    for d in range(DT):
                        last = nc.tensor.transpose(banks[0:rows, 2 * n + d // 4, d % 4 * P:(d % 4 + 1) * P], k.xT[:, d, first:first + rows], k.col("ident"))
                    last.then_inc(turned, 1)

            @block.vector
            def _(dve):
                for n, (first, rows) in enumerate(TOK):
                    dve.wait_ge(turned, n + 1)
                    nc.vector.tensor_copy(x_tm[0:rows, n, :], banks[0:rows, 2 * n:2 * n + 2, :].rearrange("p a n -> p (a n)")).then_inc(kept, 1)

            @block.sync
            def _(sp):
                sp.wait_ge(kept, 3)
                sp.dma_start(k.d["y_prompt"].rearrange("o (n p) d -> p (o n) d", p=P), x_tm[:, 0:2, :]).then_inc(stored, 16)
                sp.dma_start(k.d["y_sample"].rearrange("b t d -> (b t) d"), x_tm[0:NSAM, 2, :]).then_inc(stored, 16)
                sp.wait_ge(stored, 32)


def layer_program(nc, k):
    def sb_in(scope):
        return lambda name, shape: scope.enter_context(nc.sbuf_tensor(name, shape, F32))
    load_params(nc, k)
    rms_norm(nc, k, k.xT, "norm_mix_g", k.hh, k.hl)
    with ExitStack() as lay:
        sb = sb_in(lay)
        k.o_rwkv = sb("o_rwkv", [P, DT, T])
        k.sam_bonus, k.sam_gate = sb("sam_bonus", [P, DT, NSAM]), sb("sam_gate", [P, DT, NSAM])
        k.samT = sb("samT", [P, 6, DT, NSAM])
        with ExitStack() as rw:
            sb = sb_in(rw)
            k.gT, k.bonusT = sb("gT", [P, DT, SEQ]), sb("bonusT", [P, DT, SEQ])
            k.fT = sb("fT", [P, RT, T])
            rwkv_project(nc, k)
            k.alphaT, k.betaT = sb("alphaT", [P, DT, SEQ]), sb("betaT", [P, DT, SEQ])
            k.bendT, k.kendT = sb("bendT", [P, DT, SEQ]), sb("kendT", [P, DT, SEQ])
            k.chunk_decay = sb("chunk_decay", [P, DT, SEQ // CH])
            rwkv_prepare(nc, k)
            k.Sbd = sb("state_T", [P, DT, P])
            zero(nc, k.Sbd)
            rwkv_tile(nc, k, 0)
            rwkv_tile(nc, k, 1)
        k.o_mla = sb_in(lay)("o_mla", [P, HEADS, T])
        with ExitStack() as ml:
            sb = sb_in(ml)
            k.ckvT, k.kpe_rT = sb("ckvT", [P, 2, T]), sb("kpe_rT", [ROPE, T])
            k.kpe_tm, k.new_c = sb("kpe_tm", [P, 3, ROPE]), sb("new_c", [P, KVRANK])
            k.w_kb, k.w_vb = sb("w_kb", [P, 2, HEADS * NOPE]), sb("w_vb", [P, 2, HEADS * NOPE])
            k.qa, k.qr = sb("qa", [P, 2, NB, 32]), sb("qr", [ROPE, NB, 32])
            k.new_scores = sb("new_scores", [P, NB, 32])
            with ExitStack() as m1:
                sb = sb_in(m1)
                k.qnT, k.qrT = sb("qnT", [P, HEADS, T]), sb("qrT", [ROPE, HEADS, T])
                with ExitStack() as m2:
                    sb = sb_in(m2)
                    k.cqT = sb("cqT", [P, 4, T])
                    mla_project(nc, k)
                    k.knT, k.krT = sb("knT", [P, HEADS, SEQ]), sb("krT", [ROPE, HEADS, SEQ])
                    k.v_tm = sb("v_prompt_tm", [P, 2, HEADS * NOPE])
                    mla_qkv(nc, k)
                    mla_prompt(nc, k)
                mla_absorb(nc, k)
            sb = sb_in(ml)
            k.vec, k.vec_y = sb("vec", [P, 6, NS, 64]), sb("vec_y", [P, NS, 64])
            k.vec_sa = sb("vec_sa", [P, 64])
            k.state, k.state_tmp = sb("rwkv_state", [P, 64, 64]), sb("rwkv_state_tmp", [P, 64, 64])
            rwkv_sample_rows(nc, k)
            cache_attention(nc, k)
            rwkv_sample_out(nc, k)
        sb = sb_in(lay)
        k.yT = sb("ssd_yT", [P, DT, T])
        with ExitStack() as sd:
            sb = sb_in(sd)
            k.zT, k.xbcT, k.dtT = sb("silu_zT", [P, DT, T]), sb("xbcT", [P, CT, T]), sb("dtT", [SSD_HEADS, T])
            ssd_project(nc, k)
            k.ssm_T, k.ssm_nat = sb("prompt_ssm_T", [P, D]), sb("ssm_native", [P, NB, DT, P])
            zero(nc, k.ssm_T)
            for tile in range(3):
                ssd_tile(nc, k, tile)
        ssd_norm(nc, k)
        merge(nc, k)
    rms_norm(nc, k, k.xT, "norm_ffn_g", k.hh, k.hl)
    ffn(nc, k)


def zero(nc, buf):
    with Stage(nc) as st:
        with st.block() as block:
            @block.vector
            def _(dve):
                nc.vector.memset(buf[:, :], 0.0)


def hybrid_trunk(nc, dram):
    k = Kit(nc, dram)
    with ExitStack() as ctx:
        def sb(name, shape, dt=F32):
            return ctx.enter_context(nc.sbuf_tensor(name, shape, dt))
        k.const = sb("const", [P, NCONST])
        k.params = sb("params", [P, 4 * P])
        k.xT = sb("xT", [P, DT, T])
        k.hh, k.hl = sb("h_heads_T", [P, DT, T], F32R), sb("h_rests_T", [P, DT, T], F32R)
        k.shift_T = sb("shift_T", [P, RT, NB])
        k.sconv_T = sb("sconv_T", [P, CT, 3 * NB])
        k.fconv_T = sb("fconv_T", [P, 2 * FT, 2 * NB])
        k.dt_bias, k.a_log, k.ssd_d = (sb(n, [P, SSD_HEADS]) for n in ("dt_bias", "a_log", "ssd_d"))
        k.q_gain, k.k_gain = sb("q_gain", [P, QK]), sb("k_gain", [P, QK])
        k.pages = ctx.enter_context(nc.sbuf_tensor("page_ids", [1, NB * PAGES], I32))
        load_x(nc, k)
        with nc.Fori(0, DEPTH) as layer:
            k.layer = layer
            layer_program(nc, k)
        store_x(nc, k)


_INS = ['x_prompt', 'x_sample', 'cache_kv_latent', 'cache_k_rope', 'page_table', 'state_ssm', 'state_ssm_conv',
        'state_rwkv', 'state_rwkv_shift', 'state_ffn_conv', 'norm_mix_g', 'w_in', 'ssd_conv_w', 'ssd_conv_b',
        'ssd_dt_bias', 'ssd_a_log', 'ssd_d', 'ssd_norm_g', 'rwkv_shift_mu', 'rwkv_w0', 'rwkv_w_up', 'rwkv_a0',
        'rwkv_a_up', 'rwkv_g_up', 'rwkv_k_k', 'rwkv_k_a', 'rwkv_r_k', 'rwkv_ln_g', 'rwkv_ln_b', 'mla_q_a_g',
        'mla_w_q_b', 'mla_kv_a_g', 'mla_w_kb', 'mla_w_vb', 'mla_q_norm_g', 'mla_k_norm_g', 'w_gate', 'b_gate',
        'w_o_ssd', 'w_o_rwkv', 'w_o_mla', 'w_out', 'norm_ffn_g', 'ffn_w_up', 'ffn_conv_w', 'ffn_conv_b', 'ffn_w_down']
_OUTS = [('y_prompt', (1, SEQ, D)), ('y_sample', (NB, NS, D)),
         ('p_kv_latent', (DEPTH, 1, SEQ, KVRANK)), ('p_k_rope', (DEPTH, 1, SEQ, ROPE)),
         ('p_ssm', (DEPTH, 1, 16, 64, 128)), ('p_ssm_conv', (DEPTH, 1, 3, SSD_CONV_DIM)),
         ('p_rwkv', (DEPTH, 1, 16, 64, 64)), ('p_rwkv_shift', (DEPTH, 1, RWKV_IN)),
         ('p_ffn_conv', (DEPTH, 1, 2, 2 * D_FF)),
         ('s_kv_latent', (DEPTH, NB, NS, KVRANK)), ('s_k_rope', (DEPTH, NB, NS, ROPE)),
         ('s_ssm', (DEPTH, NB, 16, 64, 128)), ('s_ssm_conv', (DEPTH, NB, 3, SSD_CONV_DIM)),
         ('s_rwkv', (DEPTH, NB, 16, 64, 64)), ('s_rwkv_shift', (DEPTH, NB, RWKV_IN)),
         ('s_ffn_conv', (DEPTH, NB, 2, 2 * D_FF))]


def kernel(**inputs):
    import numpy as _np
    import concourse.bacc as _bacc
    from concourse import mybir as _mybir
    from concourse.bass_utils import run_bass_kernel_spmd as _run

    nc = _bacc.Bacc("TRN2", target_bir_lowering=False, num_devices=1)
    arrays, dram = {}, {}
    for name in _INS:
        a = _np.ascontiguousarray(inputs[name])
        arrays[f"in_{name}_dram"] = a
        dram[name] = nc.dram_tensor(f"in_{name}_dram", a.shape, _mybir.dt.from_np(a.dtype), kind="ExternalInput").ap()
    c = const_array()
    arrays["in_const_dram"] = c
    dram["const"] = nc.dram_tensor("in_const_dram", c.shape, _mybir.dt.float32, kind="ExternalInput").ap()
    for i, (name, shape) in enumerate(_OUTS):
        dram[name] = nc.dram_tensor(f"out_{i}_dram", shape, _mybir.dt.float32, kind="ExternalOutput").ap()
    for name, shape in (("scratch_vec", (NSAM, 6, D)), ("scratch_y", (NSAM, D))):
        dram[name] = nc.dram_tensor(name, shape, _mybir.dt.float32, kind="Internal").ap()
    hybrid_trunk(nc, dram)
    r = _run(nc, [arrays], core_ids=[0])
    return tuple(r.results[0][f"out_{i}_dram"] for i in range(len(_OUTS)))
```
